# Optimizing a Trainium2 kernel written in Bass

```python
import jax, jax.numpy as jnp
from jax import lax
import numpy as np

D_MODEL = 1024
BATCH = 1
SEQ = 1024
DEPTH = 1
DEC_BATCH = 8
DEC_SEQ = 8
PAST_LEN = 1024
PAGE_SIZE = 128

HEAD_DIM = 64
HEADS_PER_GROUP = 4
WINDOWS = (128, 512, 2048)
DILATIONS = (1, 4, 16)
N_GROUPS = len(WINDOWS)
N_ATTN_HEADS = N_GROUPS * HEADS_PER_GROUP
ATTN_WIDTH = N_ATTN_HEADS * HEAD_DIM
ATTN_OUT = HEADS_PER_GROUP * HEAD_DIM
ATTN_SCALE = HEAD_DIM ** -0.5
ROPE_THETA = 10000.0
CONV_WIDTH = 768
CONV_K = 3
IN_SPLITS = (ATTN_WIDTH, 2 * ATTN_WIDTH, 3 * ATTN_WIDTH,
             3 * ATTN_WIDTH + CONV_WIDTH, 3 * ATTN_WIDTH + 2 * CONV_WIDTH,
             3 * ATTN_WIDTH + 3 * CONV_WIDTH, 3 * ATTN_WIDTH + 3 * CONV_WIDTH + D_MODEL)
IN_WIDTH = 3 * ATTN_WIDTH + 3 * CONV_WIDTH + 2 * D_MODEL
N_KEYS = 128
N_EXPERTS = N_KEYS * N_KEYS
PEER_HEADS = 8
PEER_TOPK = 16
PEER_KEY_DIM = 256
PEER_BLOCK = 128
NORM_EPS = 1e-6

kernel_name = 'hybrid_dilated_swa_shortconv_peer_step'

def rmsnorm(x, g):
    xf = x.astype(jnp.float32)
    y = xf * lax.rsqrt(jnp.mean(xf * xf, axis=-1, keepdims=True) + NORM_EPS)
    return (y * g.astype(jnp.float32)).astype(x.dtype)

def rope(x, pos):
    half = HEAD_DIM // 2
    inv = ROPE_THETA ** (-jnp.arange(half, dtype=jnp.float32) / half)
    ang = pos.astype(jnp.float32)[:, None] * inv[None, :]
    cos = jnp.cos(ang)[None, :, None, :]
    sin = jnp.sin(ang)[None, :, None, :]
    xf = x.astype(jnp.float32)
    x1, x2 = xf[..., :half], xf[..., half:]
    return jnp.concatenate([x1 * cos - x2 * sin, x2 * cos + x1 * sin], axis=-1).astype(x.dtype)

def dilated_attn_prompt(q, k, v, dil, n_back):
    b, t, h, dh = q.shape
    n = t // dil
    blk = n_back
    nb = -(-n // blk)
    pad = nb * blk - n

    def split(a):
        a = a.reshape(b, n, dil, h, dh).transpose(0, 2, 1, 3, 4)
        a = jnp.pad(a, ((0, 0), (0, 0), (0, pad), (0, 0), (0, 0)))
        return a.reshape(b, dil, nb, blk, h, dh)

    def with_prev(a):
        prev = jnp.pad(a[:, :, :-1], ((0, 0), (0, 0), (1, 0), (0, 0), (0, 0), (0, 0)))
        return jnp.concatenate([prev, a], axis=3)

    qb = split(q)
    kb = with_prev(split(k))
    vb = with_prev(split(v))
    s = jnp.einsum('brnqhd,brnkhd->brnhqk', qb, kb, preferred_element_type=jnp.float32) * ATTN_SCALE
    qi = jnp.arange(blk)[:, None]
    ki = jnp.arange(2 * blk)[None, :]
    dist = qi + blk - ki
    key_row = (jnp.arange(nb)[:, None, None] - 1) * blk + ki[None]
    valid = (dist >= 0)[None] & (dist <= n_back)[None] & (key_row >= 0)
    s = jnp.where(valid[None, None, :, None], s, -jnp.inf)
    m = jnp.max(s, axis=-1, keepdims=True)
    p = jnp.exp(s - m)
    den = jnp.sum(p, axis=-1, keepdims=True)
    o = jnp.einsum('brnhqk,brnkhd->brnqhd', p, vb.astype(jnp.float32)) / jnp.swapaxes(den, 3, 4)
    lse = jnp.swapaxes((m + jnp.log(den))[..., 0], 3, 4)
    o = o.reshape(b, dil, nb * blk, h, dh)[:, :, :n].transpose(0, 2, 1, 3, 4).reshape(b, t, h, dh)
    lse = lse.reshape(b, dil, nb * blk, h)[:, :, :n].transpose(0, 2, 1, 3).reshape(b, t, h)
    return o, lse

def dilated_attn_sample(q, k_new, v_new, cache_kv, dil, n_back, past_len):
    l = cache_kv.shape[1]
    s_len = q.shape[1]
    new_kv = jnp.stack([k_new, v_new], axis=2).astype(cache_kv.dtype)
    full = jnp.concatenate([cache_kv, new_kv], axis=1)
    i = jnp.arange(s_len)[:, None]
    j = jnp.arange(n_back + 1)[None, :]
    back = i - j * dil
    valid = (past_len + back) >= 0
    g = full[:, jnp.clip(l + back, 0, None)]
    s = jnp.einsum('bshd,bskhd->bshk', q, g[:, :, :, 0], preferred_element_type=jnp.float32) * ATTN_SCALE
    s = jnp.where(valid[None, :, None, :], s, -jnp.inf)
    m = jnp.max(s, axis=-1, keepdims=True)
    p = jnp.exp(s - m)
    den = jnp.sum(p, axis=-1, keepdims=True)
    o = jnp.einsum('bshk,bskhd->bshd', p, g[:, :, :, 1].astype(jnp.float32)) / den
    lse = (m + jnp.log(den))[..., 0]
    return o, lse

def token_mix(h, pos, conv_prev, attend, w_in, conv_w, w_attn_o, w_conv_o, w_o):
    bsz, t, _ = h.shape
    z = h @ w_in
    q, k, v, bg, cg, hc, ga, gc = jnp.split(z, IN_SPLITS, axis=-1)
    q = rope(q.reshape(bsz, t, N_ATTN_HEADS, HEAD_DIM), pos)
    k = rope(k.reshape(bsz, t, N_ATTN_HEADS, HEAD_DIM), pos)
    v = v.reshape(bsz, t, N_ATTN_HEADS, HEAD_DIM)
    outs, lses = [], []
    for gi in range(N_GROUPS):
        sl = slice(gi * HEADS_PER_GROUP, (gi + 1) * HEADS_PER_GROUP)
        o, lse = attend(gi, q[:, :, sl], k[:, :, sl], v[:, :, sl])
        outs.append(o)
        lses.append(lse)
    wts = jax.nn.softmax(jnp.stack(lses), axis=0)
    o_attn = jnp.einsum('gbth,gbthd->bthd', wts, jnp.stack(outs)).reshape(bsz, t, ATTN_OUT).astype(h.dtype)
    u = cg * hc
    upad = jnp.concatenate([conv_prev.astype(u.dtype), u], axis=1)
    yc = conv_w[0] * upad[:, 0:t]
    for j in range(1, CONV_K):
        yc = yc + conv_w[j] * upad[:, j:j + t]
    zc = bg * yc
    mix = jax.nn.sigmoid(ga) * (o_attn @ w_attn_o) + jax.nn.sigmoid(gc) * (zc @ w_conv_o)
    return mix @ w_o, k, v, upad[:, t:]

def peer(x, w_query, sub_keys, expert_u, expert_v):
    bsz, t, d = x.shape
    n = bsz * t
    nc = -(-n // PEER_BLOCK)
    xf = jnp.pad(x.reshape(n, d), ((0, nc * PEER_BLOCK - n), (0, 0))).reshape(nc, PEER_BLOCK, d)
    half = PEER_KEY_DIM // 2

    def block(xb):
        q = (xb @ w_query).reshape(PEER_BLOCK, PEER_HEADS, 2, half)
        s1 = jnp.einsum('thd,kd->thk', q[:, :, 0], sub_keys[0], preferred_element_type=jnp.float32)
        s2 = jnp.einsum('thd,kd->thk', q[:, :, 1], sub_keys[1], preferred_element_type=jnp.float32)
        v1, i1 = lax.top_k(s1, PEER_TOPK)
        v2, i2 = lax.top_k(s2, PEER_TOPK)
        cand = (v1[..., :, None] + v2[..., None, :]).reshape(PEER_BLOCK, PEER_HEADS, PEER_TOPK * PEER_TOPK)
        cidx = (i1[..., :, None] * N_KEYS + i2[..., None, :]).reshape(PEER_BLOCK, PEER_HEADS, PEER_TOPK * PEER_TOPK)
        top_s, top_pos = lax.top_k(cand, PEER_TOPK)
        eidx = jnp.take_along_axis(cidx, top_pos, axis=-1)
        gate = jax.nn.softmax(top_s, axis=-1)
        act = jnp.einsum('td,thkd->thk', xb, expert_u[eidx], preferred_element_type=jnp.float32)
        coef = (gate * jax.nn.gelu(act)).astype(xb.dtype)
        return jnp.einsum('thk,thkd->td', coef, expert_v[eidx])

    out = lax.map(block, xf)
    return out.reshape(nc * PEER_BLOCK, d)[:n].reshape(bsz, t, d)

def decoder_layer(x, c, pos, conv_prev, attend, n1, n2, w_ada, b_ada, w_in, conv_w,
                  w_attn_o, w_conv_o, w_o, w_query, sub_keys, expert_u, expert_v):
    mod = jax.nn.silu(c) @ w_ada + b_ada
    sh1, sc1, g1, sh2, sc2, g2 = [m[:, None, :] for m in jnp.split(mod, 6, axis=-1)]
    h = rmsnorm(x, n1) * (1 + sc1) + sh1
    mo, k, v, conv_state = token_mix(h, pos, conv_prev, attend, w_in, conv_w, w_attn_o, w_conv_o, w_o)
    x = x + g1 * mo
    h = rmsnorm(x, n2) * (1 + sc2) + sh2
    x = x + g2 * peer(h, w_query, sub_keys, expert_u, expert_v)
    return x, k, v, conv_state

def setup_inputs(seed: int = 0) -> dict:
    key = jax.random.key(seed)
    ks = iter(jax.random.split(key, 32))

    def nrm(shape, scale):
        return jax.random.normal(next(ks), shape, jnp.float32) * scale

    cache_len = [min(w, PAST_LEN) for w in WINDOWS]
    return {
        'x_prompt': nrm((BATCH, SEQ, D_MODEL), 1.0),
        'x_sample': nrm((DEC_BATCH, DEC_SEQ, D_MODEL), 1.0),
        'cache_kv0': nrm((DEPTH, DEC_BATCH, cache_len[0], 2, HEADS_PER_GROUP, HEAD_DIM), 1.0),
        'cache_kv1': nrm((DEPTH, DEC_BATCH, cache_len[1], 2, HEADS_PER_GROUP, HEAD_DIM), 1.0),
        'cache_kv2': nrm((DEPTH, DEC_BATCH, cache_len[2], 2, HEADS_PER_GROUP, HEAD_DIM), 1.0),
        'state_conv': nrm((DEPTH, DEC_BATCH, CONV_K - 1, CONV_WIDTH), 1.0),
        'c_prompt': nrm((BATCH, D_MODEL), 1.0),
        'c_sample': nrm((DEC_BATCH, D_MODEL), 1.0),
        'norm1_g': 1.0 + nrm((DEPTH, D_MODEL), 0.1),
        'norm2_g': 1.0 + nrm((DEPTH, D_MODEL), 0.1),
        'norm_f_g': 1.0 + nrm((D_MODEL,), 0.1),
        'w_ada': nrm((DEPTH, D_MODEL, 6 * D_MODEL), 0.5 * D_MODEL ** -0.5),
        'b_ada': nrm((DEPTH, 6 * D_MODEL), 0.02),
        'w_in': nrm((DEPTH, D_MODEL, IN_WIDTH), D_MODEL ** -0.5),
        'conv_w': nrm((DEPTH, CONV_K, CONV_WIDTH), CONV_K ** -0.5),
        'w_attn_o': nrm((DEPTH, ATTN_OUT, D_MODEL), ATTN_OUT ** -0.5),
        'w_conv_o': nrm((DEPTH, CONV_WIDTH, D_MODEL), CONV_WIDTH ** -0.5),
        'w_o': nrm((DEPTH, D_MODEL, D_MODEL), D_MODEL ** -0.5),
        'w_query': nrm((DEPTH, D_MODEL, PEER_HEADS * PEER_KEY_DIM), D_MODEL ** -0.5),
        'sub_keys': nrm((DEPTH, 2, N_KEYS, PEER_KEY_DIM // 2), (PEER_KEY_DIM // 2) ** -0.5),
        'expert_u': nrm((DEPTH, N_EXPERTS, D_MODEL), D_MODEL ** -0.5),
        'expert_v': nrm((DEPTH, N_EXPERTS, D_MODEL), PEER_HEADS ** -0.5),
    }

def reference(x_prompt, x_sample, cache_kv0, cache_kv1, cache_kv2, state_conv, c_prompt, c_sample,
              norm1_g, norm2_g, norm_f_g, w_ada, b_ada, w_in, conv_w, w_attn_o, w_conv_o, w_o,
              w_query, sub_keys, expert_u, expert_v):
    caches = (cache_kv0, cache_kv1, cache_kv2)
    t_p = x_prompt.shape[1]
    pos_p = jnp.arange(t_p)
    pos_s = PAST_LEN + jnp.arange(x_sample.shape[1])
    yp, ys = x_prompt, x_sample
    kvp = [[] for _ in range(N_GROUPS)]
    kvs = [[] for _ in range(N_GROUPS)]
    convp, convs = [], []
    for l in range(DEPTH):
        wl = (norm1_g[l], norm2_g[l], w_ada[l], b_ada[l], w_in[l], conv_w[l], w_attn_o[l],
              w_conv_o[l], w_o[l], w_query[l], sub_keys[l], expert_u[l], expert_v[l])

        def attend_p(gi, q, k, v):
            return dilated_attn_prompt(q, k, v, DILATIONS[gi], WINDOWS[gi] // DILATIONS[gi])

        def attend_s(gi, q, k, v, l=l):
            return dilated_attn_sample(q, k, v, caches[gi][l], DILATIONS[gi],
                                       WINDOWS[gi] // DILATIONS[gi], PAST_LEN)

        conv0 = jnp.zeros((yp.shape[0], CONV_K - 1, CONV_WIDTH), yp.dtype)
        yp, kp, vp, cp = decoder_layer(yp, c_prompt, pos_p, conv0, attend_p, *wl)
        ys, ksn, vsn, cs = decoder_layer(ys, c_sample, pos_s, state_conv[l], attend_s, *wl)
        for gi in range(N_GROUPS):
            sl = slice(gi * HEADS_PER_GROUP, (gi + 1) * HEADS_PER_GROUP)
            lp = min(WINDOWS[gi], t_p)
            kvp[gi].append(jnp.stack([kp[:, t_p - lp:, sl], vp[:, t_p - lp:, sl]], axis=2))
            kvs[gi].append(jnp.stack([ksn[:, :, sl], vsn[:, :, sl]], axis=2))
        convp.append(cp)
        convs.append(cs)
    y_prompt = rmsnorm(yp, norm_f_g)
    y_sample = rmsnorm(ys, norm_f_g)
    return (y_prompt, y_sample,
            jnp.stack(kvp[0]), jnp.stack(kvp[1]), jnp.stack(kvp[2]), jnp.stack(convp),
            jnp.stack(kvs[0]), jnp.stack(kvs[1]), jnp.stack(kvs[2]), jnp.stack(convs))


_drawn_inputs = setup_inputs


def setup_inputs(seed=0):
    import zlib

    import numpy as np

    out = dict(_drawn_inputs(seed))
    spreads = {}
    factors = {'cache_kv0': 4.717, 'cache_kv1': 4.689, 'cache_kv2': 6.475, 'norm2_g': 2.784}
    for name, (base, spread) in spreads.items():
        noise = np.random.default_rng([zlib.crc32(name.encode()), seed]).standard_normal(out[name].shape)
        drawn = base * np.exp(spread * noise) if base else spread * noise
        out[name] = __import__('jax').numpy.asarray(drawn.astype(out[name].dtype))
    for name, factor in factors.items():
        out[name] = (out[name] * factor).astype(out[name].dtype)
    return out
```

```python
from contextlib import ExitStack

import concourse.bass as bass
import numpy as np
from concourse import mybir

F32 = mybir.dt.float32
BF16 = mybir.dt.bfloat16
U32 = mybir.dt.uint32
ALU = mybir.AluOpType
ACT = mybir.ActivationFunctionType
AX = mybir.AxisListType.X

P = 128
D = 1024
DC = D // P
SEQ = 1024
NSEQ = 8
NEW = 8
NS = NSEQ * NEW
TOK = SEQ + NS
PT = SEQ // P
NT = PT + 1
PAST = 1024
HD = 64
WINDOWS = (128, 512, 2048)
DILS = (1, 4, 16)
CACHE = tuple(min(w, PAST) for w in WINDOWS)
GROUPS = 3
SLOTS = 4
AW = GROUPS * SLOTS * HD
CW = 768
CT = CW // P
EPS = 1e-6
SCALE = HD ** -0.5
MASKED = -1e30
C_Q, C_K, C_V, C_B = 0, AW, 2 * AW, 3 * AW
C_GA = 3 * AW + 3 * CW
C_GC = C_GA + D
HEADS = 8
KEYS = 128
TOPK = 16
KD = 256
GELU = 2 * (2 / np.pi) ** 0.5
LOW = -3e38


def rows_of(t):
    return P if t < PT else NS


def constants():
    half = HD // 2
    inv = (10000.0 ** (-np.arange(half, dtype=np.float32) / half)).astype(np.float32)
    pos = np.concatenate([np.arange(SEQ), np.tile(PAST + np.arange(NEW), NSEQ)]).astype(np.float32)
    ang = (pos[:, None] * inv[None, :]).astype(np.float32)
    c, s = np.cos(ang), np.sin(ang)
    rope = np.concatenate([c, c, -s, s], axis=1).astype(np.float32)
    rope = np.concatenate([rope, np.zeros((NT * P - TOK, 4 * half), np.float32)])
    q = np.arange(P)[:, None, None]
    key = np.arange(P)[None, None, :]
    parts = []
    for g in (2, 1, 0):
        n = BLOCKS[g]
        back = (n - 1 - np.arange(n))[None, :, None]
        dist = back * P + q - key
        ok = (dist >= 0) & (dist <= WINDOWS[g]) & (dist % DILS[g] == 0)
        parts.append(np.where(ok, 0.0, MASKED).reshape(P, n * P))
    pmask = np.concatenate(parts, axis=1).astype(np.float32)
    row = np.arange(P)
    i = (row % NEW)[:, None]
    p = np.arange(P)[None, :]
    smask = np.zeros((2, P, SCOLS), np.float32)
    for j in range(4):
        d1 = i + CACHE[1] - (4 * p + j)
        smask[:, :, j * P:(j + 1) * P] = np.where((d1 <= WINDOWS[1]) & (d1 % DILS[1] == 0), 0.0, MASKED)
        d2 = i + CACHE[2] - (16 * (p % 64) + 4 * (p // 64) + j)
        smask[:, :, (4 + j) * P:(5 + j) * P] = np.where((d2 <= WINDOWS[2]) & (d2 % DILS[2] == 0), 0.0, MASKED)
    d0 = i + CACHE[0] - p
    smask[:, :, 8 * P:9 * P] = np.where(d0 <= WINDOWS[0], 0.0, MASKED)
    b2, i2 = np.arange(NS)[None, :] // NEW, np.arange(NS)[None, :] % NEW
    for r in range(2):
        b = (4 * r + row // 32)[:, None]
        for g in range(GROUPS):
            ok = (b2 == b) & (i2 <= i) & ((i - i2) % DILS[g] == 0)
            smask[r, :, SNEW + g * NS:SNEW + (g + 1) * NS] = np.where(ok, 0.0, MASKED)
    return {
        "rope": rope, "pmask": pmask, "smask": smask, "ident": np.eye(P, dtype=np.float32),
        "iota16": np.tile(np.arange(TOPK, dtype=np.float32), (P, 1)),
    }


BLOCKS = tuple(min(w // P, PT - 1) + 1 for w in WINDOWS)
SBLK = 9
SNEW = SBLK * P
SCOLS = SNEW + GROUPS * NS


def key_blocks(t):
    return [(g, kb) for g in (2, 1, 0) for kb in range(max(0, t - BLOCKS[g] + 1), t + 1)]


MASK_AT = {2: 0, 1: BLOCKS[2], 0: BLOCKS[2] + BLOCKS[1]}


def mask_block(g, t, kb):
    return MASK_AT[g] + BLOCKS[g] - 1 - (t - kb)


class Names:

    def __init__(self, nc, ctx, name):
        self.nc, self.ctx, self.name, self.used = nc, ctx, name, []
        ctx.callback(self.release)

    def release(self):
        if self.used:
            self.nc.clear_and_free_semaphores(self.used)
            self.nc.all_engine_barrier()

    def sb(self, name, shape, dt=F32):
        return self.ctx.enter_context(self.nc.sbuf_tensor(f"{self.name}_{name}", shape, dt))

    def ps(self, name, shape, dt=F32):
        return self.ctx.enter_context(self.nc.psum_tensor(f"{self.name}_{name}", shape, dt))

    def sem(self, name):
        self.used.append(self.nc.alloc_semaphore(f"{self.name}_{name}"))
        return self.used[-1]

    def sems(self, name, n):
        return [self.sem(f"{name}{i}") for i in range(n)]


def rep_rows(src, row0, rows, reps, stride, col, n):
    return bass.AP(src.tensor, src.offset + row0 * stride + col, [[stride, rows], [0, reps], [1, n]])


def ada(nc, io, keep):
    with ExitStack() as ctx:
        n = Names(nc, ctx, "ada")
        NQ = 1 + NSEQ
        W, NG, RING = 512, 6 * D // 512, 3
        c, e, sc = n.sb("c", [NQ, D]), n.sb("e", [NQ, D]), n.sb("silu", [NQ, D])
        cT = n.sb("cT", [P, DC, NQ])
        bias, mod = n.sb("bias", [NQ, 6 * D]), n.sb("mod", [NQ, 6 * D])
        gains = n.sb("gains", [NQ, 2, D])
        w = n.sb("w", [P, RING, DC, W])
        psT, psM = n.ps("psT", [P, 512]), n.ps("psM", [P, 2, 512])
        loaded, consts = n.sem("c_loaded"), n.sem("rows_loaded")
        w_in = n.sems("w_loaded", RING)
        exp_done, silu_done, tr_done, cT_done = n.sem("exp"), n.sem("silu_s"), n.sem("tr"), n.sem("cT_s")
        mm_done, added, scaled, stored = n.sem("mm"), n.sem("added"), n.sem("scaled"), n.sem("stored")
        w_v = io["w_ada"].rearrange("(c p) n -> p c n", p=P)
        block = ctx.enter_context(nc.Block())

        @block.sync
        def _(sp):
            sp.dma_start(c[0:1, :], io["c_prompt"]).then_inc(loaded, 16)
            sp.dma_start(c[1:NQ, :], io["c_sample"]).then_inc(loaded, 16)
            sp.dma_start(keep["ident"][:], io["ident"]).then_inc(loaded, 16)
            for g in range(NG):
                if g >= RING:
                    sp.wait_ge(mm_done, g - RING + 1)
                sp.dma_start(w[:, g % RING], w_v[:, :, g * W:(g + 1) * W]).then_inc(w_in[g % RING], 16)
                if g == 0:
                    sp.dma_start(bias[:], io["b_ada"].broadcast_to([NQ, 6 * D])).then_inc(consts, 16)
                    sp.dma_start(gains[:, 0, :], io["norm1_g"].broadcast_to([NQ, D])).then_inc(consts, 16)
                    sp.dma_start(gains[:, 1, :], io["norm2_g"].broadcast_to([NQ, D])).then_inc(consts, 16)
            sp.wait_ge(scaled, 2)
            sp.wait_ge(added, NG)
            sp.dma_start(io["mod"], mod[:]).then_inc(stored, 16)
            sp.wait_ge(stored, 16)

        @block.scalar
        def _(act):
            act.wait_ge(loaded, 48)
            act.activation(e[:], c[:], ACT.Exp, scale=-1.0).then_inc(exp_done, 1)

        @block.tensor
        def _(pe):
            pe.wait_ge(silu_done, 3)
            for k in range(DC):
                last = pe.transpose(psT[:, k * NQ:(k + 1) * NQ], sc[:, k * P:(k + 1) * P],
                                    keep["ident"][0:NQ, 0:NQ])
            last.then_inc(tr_done, 1)
            pe.wait_ge(cT_done, 1)
            for g in range(NG):
                pe.wait_ge(w_in[g % RING], 16 * (g // RING + 1))
                if g >= 2:
                    pe.wait_ge(added, g - 1)
                for k in range(DC):
                    last = pe.matmul(psM[0:NQ, g % 2, :], cT[:, k, :], w[:, g % RING, k, :],
                                     start=(k == 0), stop=(k == DC - 1))
                last.then_inc(mm_done, 1)

        @block.vector
        def _(dve):
            dve.wait_ge(exp_done, 1)
            dve.tensor_scalar(e[:], e[:], 1.0, None, ALU.add).then_inc(silu_done, 1)
            dve.wait_ge(silu_done, 1)
            dve.reciprocal(sc[:], e[:]).then_inc(silu_done, 1)
            dve.wait_ge(silu_done, 2)
            dve.tensor_tensor(sc[:], sc[:], c[:], ALU.mult).then_inc(silu_done, 1)
            dve.wait_ge(tr_done, 1)
            dve.tensor_copy(cT[:].rearrange("p c n -> p (c n)"), psT[:, 0:DC * NQ]).then_inc(cT_done, 1)
            dve.wait_ge(consts, 48)
            for g in range(NG):
                dve.wait_ge(mm_done, g + 1)
                dve.tensor_tensor(mod[:, g * W:(g + 1) * W], psM[0:NQ, g % 2, :], bias[:, g * W:(g + 1) * W],
                                  ALU.add).then_inc(added, 1)
            dve.wait_ge(added, NG)
            for i, at in enumerate((D, 4 * D)):
                dve.scalar_tensor_tensor(out=mod[:, at:at + D], in0=mod[:, at:at + D], scalar=1.0,
                                         in1=gains[:, i, :], op0=ALU.add, op1=ALU.mult).then_inc(scaled, 1)


def load_rows(eng, io, dst, t, col, sem):
    if t < PT:
        src = rep_rows(io["mod"], 0, 1, P, 6 * D, col, D)
    else:
        src = rep_rows(io["mod"], 1, NSEQ, NEW, 6 * D, col, D)
    return eng.dma_start(dst[0:rows_of(t), :], src).then_inc(sem, 16)


def norm(nc, io, keep):
    with ExitStack() as ctx:
        n = Names(nc, ctx, "norm")
        XR = 3
        x, m, h = n.sb("x", [P, XR, D]), n.sb("m", [P, 2, D]), n.sb("h", [P, 2, D])
        sq = n.sb("sq", [P, D])
        gain, shift = n.sb("gain", [P, 2, D]), n.sb("shift", [P, 2, D])
        ss, rt, rs = n.sb("ss", [P, NT]), n.sb("rt", [P, NT]), n.sb("rs", [P, NT])
        psT = n.ps("psT", [P, 2, DC * P])
        x_in, rows_in = n.sems("x_loaded", XR), n.sem("rows_loaded")
        squared, rooted, inverted = n.sem("squared"), n.sem("rooted"), n.sem("inverted")
        scaled, shifted, turned, kept = n.sem("scaled"), n.sem("shifted"), n.sem("turned"), n.sem("kept")
        eps, eps_set = n.sb("eps", [P, 1]), n.sem("eps_set")
        hT = keep["hT"]
        block = ctx.enter_context(nc.Block())

        @block.sync
        def _(sp):
            for t in range(NT):
                R = rows_of(t)
                if t >= XR:
                    sp.wait_ge(scaled, t - XR + 1)
                src = io["x_prompt"][t * P:t * P + R, :] if t < PT else io["x_sample"]
                sp.dma_start(x[0:R, t % XR, :], src).then_inc(x_in[t % XR], 16)
                if t == 0:
                    for i, tt in enumerate((0, PT)):
                        load_rows(sp, io, gain[:, i, :], tt, D, rows_in)
                        load_rows(sp, io, shift[:, i, :], tt, 0, rows_in)

        @block.gpsimd
        def _(pool):
            pool.memset(eps[:], EPS).then_inc(eps_set, 1)

        def keep_turned(act, t):
            R = rows_of(t)
            act.wait_ge(turned, t + 1)
            for i in range(2):
                src = psT[:, t % 2, i * 512:i * 512 + 4 * P].rearrange("p (c r) -> p c r", r=P)[:, :, 0:R]
                act.activation(hT[:, 4 * i:4 * i + 4, t * P:t * P + R], src, ACT.Copy).then_inc(kept, 1)

        @block.scalar
        def _(act):
            act.wait_ge(eps_set, 1)
            for t in range(NT):
                R = rows_of(t)
                act.wait_ge(x_in[t % XR], 16 * (t // XR + 1))
                if t:
                    act.wait_ge(squared, t)
                act.activation(sq[0:R, :], x[0:R, t % XR, :], ACT.Square,
                               accum_out=ss[0:R, t:t + 1]).then_inc(squared, 1)
                act.wait_ge(squared, t + 1)
                act.activation(rt[0:R, t:t + 1], ss[0:R, t:t + 1], ACT.Sqrt, bias=eps[0:R, :],
                               scale=1.0 / D).then_inc(rooted, 1)
                if t:
                    keep_turned(act, t - 1)
            keep_turned(act, NT - 1)

        @block.vector
        def _(dve):
            dve.wait_ge(rows_in, 64)
            for t in range(NT):
                R, i = rows_of(t), t // PT
                dve.wait_ge(rooted, t + 1)
                dve.reciprocal(rs[0:R, t:t + 1], rt[0:R, t:t + 1]).then_inc(inverted, 1)
                dve.wait_ge(inverted, t + 1)
                dve.scalar_tensor_tensor(out=m[0:R, t % 2, :], in0=x[0:R, t % XR, :], scalar=rs[0:R, t:t + 1],
                                         in1=gain[0:R, i, :], op0=ALU.mult, op1=ALU.mult).then_inc(scaled, 1)
                dve.wait_ge(scaled, t + 1)
                if t >= 2:
                    dve.wait_ge(turned, t - 1)
                dve.tensor_tensor(h[0:R, t % 2, :], m[0:R, t % 2, :], shift[0:R, i, :],
                                  ALU.add).then_inc(shifted, 1)

        @block.tensor
        def _(pe):
            for t in range(NT):
                R = rows_of(t)
                pe.wait_ge(shifted, t + 1)
                if t >= 2:
                    pe.wait_ge(kept, 2 * (t - 1))
                for k in range(DC):
                    last = pe.transpose(psT[:, t % 2, k * P:k * P + R], h[0:R, t % 2, k * P:(k + 1) * P],
                                        keep["ident"][0:R, 0:R])
                last.then_inc(turned, 1)


def qkv(nc, io, keep):
    with ExitStack() as ctx:
        n = Names(nc, ctx, "qkv")
        W, RING, ROT = 384, 3, 4
        HB = W // HD
        NG = 3 * AW // W
        NR = 4 * NT
        w = n.sb("w", [P, RING, DC, W])
        rope = n.sb("rope", [P, NT, 4 * (HD // 2)])
        m1, m2 = n.sb("m1", [P, 2, W]), n.sb("m2", [P, 2, W])
        rot = n.sb("rot", [P, ROT, W])
        psZ, psT = n.ps("psZ", [P, 3, 512]), n.ps("psT", [P, 2, 512])
        w_in, rope_in = n.sems("w_loaded", RING), n.sem("rope_loaded")
        z_done, m_done, rot_done = n.sem("z"), n.sem("m"), n.sem("rotated")
        v_kept, turned, kept = n.sem("v_kept"), n.sem("turned"), n.sem("kept")
        stored, v_stored = n.sems("stored", ROT), n.sem("v_stored")
        hT, V, Vs = keep["hT"], keep["V"], keep["Vs"]
        w_v = io["w_in"].rearrange("(c p) n -> p c n", p=P)

        def heads(g):
            a, b = (g % 2) * W, (g % 2 + 1) * W
            return [(j, max(a, j * 256), min(b, (j + 1) * 256)) for j in range(GROUPS)
                    if max(a, j * 256) < min(b, (j + 1) * 256)]

        def store(eng, kv, t, j, a, b, src, sem):
            if t == PT:
                dst = io["kvs"][j][:, kv, a - j * 256:b - j * 256]
            else:
                first = (t * P) - (SEQ - CACHE_OUT[j])
                if first < 0:
                    return 0
                dst = io["kvp"][j][first:first + P, kv, a - j * 256:b - j * 256]
            eng.dma_start(dst, src).then_inc(sem, 16)
            return 1

        CACHE_OUT = tuple(min(x, SEQ) for x in WINDOWS)
        reads = [0] * ROT
        k_stores = {}
        for i in range(NR):
            g, t = divmod(i, NT)
            if g >= 2:
                reads[i % ROT] += sum(t == PT or t * P >= SEQ - CACHE_OUT[j] for j, _, _ in heads(g))
            k_stores[i] = reads[i % ROT]
        block = ctx.enter_context(nc.Block())

        @block.sync
        def _(sp):
            for g in range(NG):
                if g >= RING:
                    sp.wait_ge(z_done, NT * (g - RING + 1))
                sp.dma_start(w[:, g % RING], w_v[:, :, g * W:(g + 1) * W]).then_inc(w_in[g % RING], 16)
                if g == 0:
                    sp.dma_start(rope[:], io["rope"].rearrange("(t p) c -> p t c", p=P)).then_inc(rope_in, 16)

        @block.gpsimd
        def _(pool):
            for i in range(2 * NT, NR):
                g, t = divmod(i, NT)
                R = rows_of(t)
                pool.wait_ge(rot_done, i + 1)
                for j, a, b in heads(g):
                    at = a - (g % 2) * W
                    store(pool, 0, t, j, a, b, rot[0:R, i % ROT, at:at + b - a], stored[i % ROT])
            count = 0
            pool.wait_ge(v_kept, 2 * NT)
            for t in range(NT):
                R = rows_of(t)
                for j in range(GROUPS):
                    src = V[:, t, j * 256:(j + 1) * 256] if t < PT else Vs[:, j * 256:(j + 1) * 256]
                    count += store(pool, 1, t, j, j * 256, (j + 1) * 256, src, v_stored)
            for r in range(ROT):
                pool.wait_ge(stored[r], 16 * reads[r])
            pool.wait_ge(v_stored, 16 * count)

        @block.tensor
        def _(pe):
            def turn(i):
                g, t = divmod(i, NT)
                R = rows_of(t)
                pe.wait_ge(rot_done, i + 1)
                if i >= 2:
                    pe.wait_ge(kept, i - 1)
                for j in range(3):
                    last = pe.transpose(psT[:, i % 2, j * P:j * P + R], rot[0:R, i % ROT, j * P:(j + 1) * P],
                                        keep["ident"][0:R, 0:R])
                last.then_inc(turned, 1)

            for i in range(NG * NT):
                g, t = divmod(i, NT)
                R = rows_of(t)
                if t == 0:
                    pe.wait_ge(w_in[g % RING], 16 * (g // RING + 1))
                if i >= 3:
                    if i - 3 < NR:
                        pe.wait_ge(m_done, 3 * (i - 2))
                    else:
                        pe.wait_ge(v_kept, i - 2 - NR)
                for k in range(DC):
                    last = pe.matmul(psZ[0:R, i % 3, 0:W], hT[:, k, t * P:t * P + R], w[:, g % RING, k, :],
                                     start=(k == 0), stop=(k == DC - 1))
                last.then_inc(z_done, 1)
                if 1 <= i <= NR:
                    turn(i - 1)

        @block.vector
        def _(dve):
            dve.wait_ge(rope_in, 16)
            H = HD // 2
            for i in range(NR):
                g, t = divmod(i, NT)
                R = rows_of(t)
                z = psZ[0:R, i % 3, 0:W].rearrange("p (h d) -> p h d", d=HD)
                a = m1[0:R, i % 2, :].rearrange("p (h d) -> p h d", d=HD)
                b = m2[0:R, i % 2, :].rearrange("p (h d) -> p h d", d=HD)
                cos = rope[0:R, t:t + 1, 0:HD].broadcast_to([R, HB, HD])
                nsin = rope[0:R, t:t + 1, HD:HD + H].broadcast_to([R, HB, H])
                sin = rope[0:R, t:t + 1, HD + H:2 * HD].broadcast_to([R, HB, H])
                dve.wait_ge(z_done, i + 1)
                if i >= 2:
                    dve.wait_ge(rot_done, i - 1)
                dve.tensor_tensor(a, z, cos, ALU.mult).then_inc(m_done, 1)
                dve.tensor_tensor(b[:, :, 0:H], z[:, :, H:HD], nsin, ALU.mult).then_inc(m_done, 1)
                dve.tensor_tensor(b[:, :, H:HD], z[:, :, 0:H], sin, ALU.mult).then_inc(m_done, 1)
                dve.wait_ge(m_done, 3 * (i + 1))
                if i >= ROT:
                    dve.wait_ge(turned, i - ROT + 1)
                    if k_stores[i - ROT]:
                        dve.wait_ge(stored[i % ROT], 16 * k_stores[i - ROT])
                dve.tensor_tensor(rot[0:R, i % ROT, :], m1[0:R, i % 2, :], m2[0:R, i % 2, :],
                                  ALU.add).then_inc(rot_done, 1)

        @block.scalar
        def _(act):
            for i in range(NR):
                g, t = divmod(i, NT)
                R = rows_of(t)
                full, samp = (keep["qT"], keep["qTs"]) if g < 2 else (keep["kT"], keep["kTs"])
                pr = 3 * (g % 2)
                src = psT[:, i % 2, 0:3 * P].rearrange("p (j r) -> p j r", r=P)[:, :, 0:R]
                dst = full[:, pr:pr + 3, t * P:(t + 1) * P] if t < PT else samp[:, pr:pr + 3, :]
                act.wait_ge(turned, i + 1)
                act.activation(dst, src, ACT.Copy).then_inc(kept, 1)
            for i in range(NR, NG * NT):
                g, t = divmod(i, NT)
                R = rows_of(t)
                at = (g - 4) * W
                dst = V[:, t, at:at + W] if t < PT else Vs[:, at:at + W]
                act.wait_ge(z_done, i + 1)
                act.activation(dst, psZ[0:R, i % 3, 0:W], ACT.Copy).then_inc(v_kept, 1)


def attend(nc, io, keep):
    with ExitStack() as ctx:
        n = Names(nc, ctx, "att")
        NI = PT * SLOTS
        NB = sum(BLOCKS)
        TR = 4
        maskf, mask, identb = n.sb("maskf", [P, NB * P]), n.sb("mask", [P, NB * P], BF16), n.sb("identb", [P, P], BF16)
        prob = n.sb("prob", [P, 2, NB * P])
        pT = n.sb("pT", [P, TR, 4 * P])
        o = n.sb("o", [P, 2, SLOTS * HD])
        mx, nm, den, rden = (n.sb(x, [P, NI]) for x in ("mx", "nm", "den", "rden"))
        psS, psT, psO = n.ps("psS", [P, 4 * 512]), n.ps("psT", [P, 2, 512]), n.ps("psO", [P, 2, 512])
        mask_in, mask_set = n.sem("mask_loaded"), n.sem("mask_set")
        scored, maxed, negated, expd = n.sem("scored"), n.sem("maxed"), n.sem("negated"), n.sem("exp")
        inverted, turned, kept, summed = n.sem("inverted"), n.sem("turned"), n.sem("kept"), n.sem("summed")
        scaled, o_turned, o_kept = n.sem("scaled"), n.sem("o_turned"), n.sem("o_kept")
        qT, kT, V, oT, ident = keep["qT"], keep["kT"], keep["V"], keep["oT"], keep["ident"]
        blocks = [key_blocks(it // SLOTS) for it in range(NI)]
        first = [0]
        for b in blocks:
            first.append(first[-1] + -(-len(b) // 4))
        block = ctx.enter_context(nc.Block())

        @block.sync
        def _(sp):
            sp.dma_start(maskf[:], io["pmask"]).then_inc(mask_in, 16)

        @block.tensor
        def _(pe):
            def scores(it):
                t, h = divmod(it, SLOTS)
                lane = HD * (h % 2)
                if it:
                    pe.wait_ge(expd, it)
                bl, at = blocks[it], 0
                while at < len(bl):
                    g, kb = bl[at]
                    run = 1
                    while at + run < len(bl) and bl[at + run][0] == g and (at + run) % 4:
                        run += 1
                    dst = psS[:, at * P:(at + run) * P]
                    m0 = mask_block(g, t, kb)
                    pe.matmul(dst, identb[:], mask[:, m0 * P:(m0 + run) * P], start=True, stop=False)
                    pair = 2 * g + h // 2
                    last = pe.matmul(dst, qT[lane:lane + HD, pair, t * P:(t + 1) * P],
                                     kT[lane:lane + HD, pair, kb * P:(kb + run) * P], start=False, stop=True)
                    at += run
                last.then_inc(scored, 1)

            def outputs(it):
                t, h = divmod(it, SLOTS)
                bl = blocks[it]
                NBT = first[it + 1] - first[it]
                pe.wait_ge(expd, it + 1)

                def turn(j):
                    b = first[it] + j
                    if b >= 2:
                        pe.wait_ge(kept, b - 1)
                    for i in range(4 * j, min(4 * j + 4, len(bl))):
                        last = pe.transpose(psT[:, b % 2, (i % 4) * P:(i % 4 + 1) * P],
                                            prob[:, it % 2, i * P:(i + 1) * P], ident[:])
                    last.then_inc(turned, 1)

                def weigh(j):
                    b = first[it] + j
                    pe.wait_ge(kept, b + 1)
                    if it >= 2 and j == 0:
                        pe.wait_ge(scaled, it - 1)
                        if it % 2 and t and h == 1:
                            pe.wait_ge(o_kept, t)
                    for i in range(4 * j, min(4 * j + 4, len(bl))):
                        g, kb = bl[i]
                        last = pe.matmul(psO[:, it % 2, 0:HD], pT[:, b % TR, (i % 4) * P:(i % 4 + 1) * P],
                                         V[:, kb, (g * SLOTS + h) * HD:(g * SLOTS + h + 1) * HD],
                                         start=(i == 0), stop=(i == len(bl) - 1))
                    last.then_inc(summed, 1)

                for j in range(NBT + 2):
                    if j < NBT:
                        turn(j)
                    if j >= 2:
                        weigh(j - 2)

            def turn_o(t):
                pe.wait_ge(scaled, SLOTS * (t + 1))
                for j in range(2):
                    last = pe.transpose(psO[:, 1, j * P:(j + 1) * P], o[:, t % 2, j * P:(j + 1) * P],
                                        ident[:])
                last.then_inc(o_turned, 1)

            pe.wait_ge(mask_set, 2)
            scores(0)
            for it in range(NI):
                if it + 1 < NI:
                    scores(it + 1)
                outputs(it)
                if it >= 1 and (it - 1) % SLOTS == SLOTS - 1:
                    turn_o((it - 1) // SLOTS)
            turn_o(PT - 1)

        @block.vector
        def _(dve):
            dve.wait_ge(mask_in, 16)
            dve.tensor_copy(mask[:], maskf[:]).then_inc(mask_set, 1)
            dve.tensor_copy(identb[:], ident[:]).then_inc(mask_set, 1)

            def top(it):
                dve.wait_ge(scored, it + 1)
                dve.tensor_reduce(mx[:, it:it + 1], psS[:, 0:len(blocks[it]) * P], AX, ALU.max).then_inc(maxed, 1)
                dve.wait_ge(maxed, it + 1)
                dve.tensor_scalar(nm[:, it:it + 1], mx[:, it:it + 1], -SCALE, None, ALU.mult).then_inc(negated, 1)

            top(0)
            for it in range(NI):
                if it + 1 < NI:
                    top(it + 1)
                dve.wait_ge(expd, it + 1)
                dve.reciprocal(rden[:, it:it + 1], den[:, it:it + 1]).then_inc(inverted, 1)
                for b in range(first[it], first[it + 1]):
                    m = min(4, len(blocks[it]) - 4 * (b - first[it]))
                    dve.wait_ge(turned, b + 1)
                    if b >= TR:
                        dve.wait_ge(summed, b - TR + 1)
                    dve.tensor_copy(pT[:, b % TR, 0:m * P], psT[:, b % 2, 0:m * P]).then_inc(kept, 1)

        @block.scalar
        def _(act):
            def exps(it):
                act.wait_ge(negated, it + 1)
                m = len(blocks[it]) * P
                if it >= 2:
                    act.wait_ge(turned, first[it - 1])
                act.activation(prob[:, it % 2, 0:m], psS[:, 0:m], ACT.Exp, bias=nm[:, it:it + 1], scale=SCALE,
                               accum_out=den[:, it:it + 1]).then_inc(expd, 1)

            def keep_o(t):
                act.wait_ge(o_turned, t + 1)
                act.activation(oT[:, :, t * P:(t + 1) * P],
                               psO[:, 1, 0:2 * P].rearrange("p (j r) -> p j r", r=P),
                               ACT.Copy).then_inc(o_kept, 1)

            exps(0)
            for it in range(NI):
                if it + 1 < NI:
                    exps(it + 1)
                t, h = divmod(it, SLOTS)
                act.wait_ge(summed, first[it + 1])
                act.wait_ge(inverted, it + 1)
                if t >= 2 and h == 0:
                    act.wait_ge(o_turned, t - 1)
                act.activation(o[:, t % 2, h * HD:(h + 1) * HD], psO[:, it % 2, 0:HD], ACT.Copy,
                               scale=rden[:, it:it + 1]).then_inc(scaled, 1)
                if it >= 1 and (it - 1) % SLOTS == SLOTS - 1:
                    keep_o((it - 1) // SLOTS)
            keep_o(PT - 1)


def sampled(nc, io, keep):
    with ExitStack() as ctx:
        n = Names(nc, ctx, "smp")
        QB = 4
        NB6 = 6
        K, Vc = n.sb("K", [P, 2, SBLK, 256]), n.sb("Vc", [P, QB, SBLK, 256])
        kTc = n.sb("kTc", [P, 2, 2, SNEW])
        qz = n.sb("qz", [P, GROUPS, QB, 2, P])
        mask, S, pr = n.sb("mask", [P, SCOLS]), n.sb("S", [P, SCOLS]), n.sb("pr", [P, SCOLS])
        pT = n.sb("pT", [P, SBLK + GROUPS, P])
        mx, nm, den, rden = (n.sb(x, [P, 2]) for x in ("mx", "nm", "den", "rden"))
        psS, psT, psO = n.ps("psS", [P, 4 * 512]), n.ps("psT", [P, 3, 512]), n.ps("psO", [P, 512])
        k_in, v_in, mask_in = n.sems("k_loaded", 2), n.sems("v_loaded", QB), n.sem("mask_loaded")
        q_clear, q_set = n.sem("q_clear"), n.sem("q_set")
        k_turned, k_kept, scored = n.sem("k_turned"), n.sem("k_kept"), n.sem("scored")
        scored_part = n.sem("scored_part")
        masked, maxed, negated, expd = n.sem("masked"), n.sem("maxed"), n.sem("negated"), n.sem("exp")
        inverted, normed, p_turned, p_kept = n.sem("inverted"), n.sem("normed"), n.sem("p_turned"), n.sem("p_kept")
        summed, o_kept = n.sem("summed"), n.sem("o_kept")
        qTs, kTs, Vs, oT, ident = keep["qTs"], keep["kTs"], keep["Vs"], keep["oT"], keep["ident"]
        BG = [1] * 4 + [2] * 4 + [0]

        def load(eng, b, kv, dst, sem):
            c0, c1, c2 = io["cache"]
            eng.dma_start(dst[:, 0:4, :], c1[b, :, kv, :].rearrange("(p j) c -> p j c", j=4)).then_inc(sem, 16)
            for s in range(2):
                src = bass.AP(c2.tensor, c2.offset + ((b * CACHE[2] + 4 * s) * 2 + kv) * 256,
                              [[16 * 512, 64], [512, 4], [1, 256]])
                eng.dma_start(dst[64 * s:64 * s + 64, 4:8, :], src).then_inc(sem, 16)
            eng.dma_start(dst[:, 8, :], c0[b, :, kv, :]).then_inc(sem, 16)

        block = ctx.enter_context(nc.Block())
        TB = 3

        @block.sync
        def _(sp):
            for b in range(NSEQ):
                if b >= 2:
                    sp.wait_ge(k_turned, NB6 * (b - 1))
                load(sp, b, 0, K[:, b % 2], k_in[b % 2])
                if b % QB == 0:
                    r = b // QB
                    if r:
                        sp.wait_ge(masked, 2)
                    sp.dma_start(mask[:], io["smask"][r]).then_inc(mask_in, 16)

        @block.gpsimd
        def _(pool):
            pool.memset(qz[:], 0.0).then_inc(q_clear, 1)
            pool.wait_ge(q_clear, 1)
            for r in range(2):
                if r:
                    pool.wait_ge(scored, 1)
                for g in range(GROUPS):
                    for b in range(QB):
                        for h in range(SLOTS):
                            lane, pair = HD * (h % 2), h // 2
                            at = b * 32 + h * NEW
                            tok = (QB * r + b) * NEW
                            pool.tensor_copy(qz[lane:lane + HD, g, b, pair, at:at + NEW],
                                             qTs[lane:lane + HD, 2 * g + pair, tok:tok + NEW]).then_inc(q_set, 1)
                for b in range(QB):
                    if r:
                        pool.wait_ge(summed, 1)
                    load(pool, QB * r + b, 1, Vc[:, b], v_in[b])

        @block.tensor
        def _(pe):
            def turn_keys(b):
                pe.wait_ge(k_in[b % 2], 64 * (b // 2 + 1))
                for pair in range(2):
                    for j in range(3):
                        i = NB6 * b + 3 * pair + j
                        if i >= 3:
                            pe.wait_ge(k_kept, i - 2)
                        for k in range(4 * j, min(4 * j + 4, SBLK)):
                            last = pe.transpose(psT[:, i % 3, (k % 4) * P:(k % 4 + 1) * P],
                                                K[:, b % 2, k, pair * P:(pair + 1) * P], ident[:])
                        last.then_inc(k_turned, 1)

            def scores(b):
                q, r = b % QB, b // QB
                pe.wait_ge(k_kept, NB6 * (b + 1))
                if q == 0:
                    pe.wait_ge(q_set, 48 * (r + 1))
                    if r:
                        pe.wait_ge(masked, 2)
                for pair in range(2):
                    for at, m, g in ((0, 4, 1), (4, 4, 2), (8, 1, 0)):
                        last = pe.matmul(psS[:, at * P:(at + m) * P], qz[:, g, q, pair, :],
                                         kTc[:, b % 2, pair, at * P:(at + m) * P],
                                         start=(q == 0 and pair == 0), stop=(q == QB - 1 and pair == 1))
                if q == QB - 1:
                    for g in range(GROUPS):
                        for q2 in range(QB):
                            for pair in range(2):
                                last = pe.matmul(psS[:, 3 * 512 + g * NS:3 * 512 + (g + 1) * NS],
                                                 qz[:, g, q2, pair, :], kTs[:, 2 * g + pair, :],
                                                 start=(q2 == 0 and pair == 0), stop=(q2 == QB - 1 and pair == 1))
                    last.then_inc(scored, 1)
                else:
                    last.then_inc(scored_part, 1)

            def outputs(r):
                pe.wait_ge(normed, r + 1)
                for j in range(TB):
                    if j == 0:
                        pe.wait_ge(k_kept, NB6 * QB * (r + 1))
                    for k in range(4 * j, 4 * j + 4):
                        if k < SBLK:
                            last = pe.transpose(psT[:, j, (k % 4) * P:(k % 4 + 1) * P], pr[:, k * P:(k + 1) * P],
                                                ident[:])
                        else:
                            g = k - SBLK
                            last = pe.transpose(psT[0:NS, j, (k % 4) * P:(k % 4 + 1) * P],
                                                pr[:, SNEW + g * NS:SNEW + (g + 1) * NS], ident[:])
                    last.then_inc(p_turned, 1)
                pe.wait_ge(p_kept, (TB + 1) * (r + 1))
                if r:
                    pe.wait_ge(o_kept, 4)
                for q in range(QB):
                    pe.wait_ge(v_in[q], 64 * (r + 1))
                    for pair in range(2):
                        dst = psO[:, (2 * q + pair) * 32:(2 * q + pair + 1) * 32]
                        for k in range(SBLK):
                            pe.matmul(dst, Vc[:, q, k, pair * P:(pair + 1) * P], pT[:, k, q * 32:(q + 1) * 32],
                                      start=(k == 0), stop=False)
                        for g in range(GROUPS):
                            last = pe.matmul(dst, Vs[:, g * 256 + pair * P:g * 256 + (pair + 1) * P],
                                             pT[0:NS, SBLK + g, q * 32:(q + 1) * 32],
                                             start=False, stop=(g == GROUPS - 1))
                last.then_inc(summed, 1)

            for r in range(2):
                turn_keys(QB * r)
                for b in range(QB * r, QB * r + QB):
                    if b + 1 < QB * r + QB:
                        turn_keys(b + 1)
                    scores(b)
                outputs(r)

        @block.vector
        def _(dve):
            for r in range(2):
                for b in range(QB * r, QB * r + QB):
                    if b >= 2:
                        dve.wait_ge(scored_part, (b - 2) // QB * (QB - 1) + min((b - 2) % QB + 1, QB - 1))
                        if b >= QB + 1:
                            dve.wait_ge(scored, 1)
                    for pair in range(2):
                        for j in range(3):
                            i = NB6 * b + 3 * pair + j
                            m = 4 if j < 2 else 1
                            dve.wait_ge(k_turned, i + 1)
                            dve.tensor_copy(kTc[:, b % 2, pair, 4 * j * P:(4 * j + m) * P],
                                            psT[:, i % 3, 0:m * P]).then_inc(k_kept, 1)
                dve.wait_ge(scored, r + 1)
                dve.wait_ge(mask_in, 16 * (r + 1))
                if r:
                    dve.wait_ge(expd, r)
                dve.tensor_tensor(S[:, 0:SNEW], psS[:, 0:SNEW], mask[:, 0:SNEW], ALU.add).then_inc(masked, 1)
                dve.tensor_tensor(S[:, SNEW:SCOLS], psS[:, 3 * 512:3 * 512 + GROUPS * NS], mask[:, SNEW:SCOLS],
                                  ALU.add).then_inc(masked, 1)
                dve.wait_ge(masked, 2 * (r + 1))
                dve.tensor_reduce(mx[:, r:r + 1], S[:], AX, ALU.max).then_inc(maxed, 1)
                dve.wait_ge(maxed, r + 1)
                dve.tensor_scalar(nm[:, r:r + 1], mx[:, r:r + 1], -SCALE, None, ALU.mult).then_inc(negated, 1)
                dve.wait_ge(expd, r + 1)
                dve.reciprocal(rden[:, r:r + 1], den[:, r:r + 1]).then_inc(inverted, 1)
                dve.wait_ge(inverted, r + 1)
                dve.tensor_scalar(pr[:], pr[:], rden[:, r:r + 1], None, ALU.mult).then_inc(normed, 1)
                for j in range(TB):
                    dve.wait_ge(p_turned, TB * r + j + 1)
                    if j < 2:
                        dve.tensor_copy(pT[:, 4 * j:4 * j + 4, :].rearrange("p j c -> p (j c)"),
                                        psT[:, j, :]).then_inc(p_kept, 1)
                    else:
                        dve.tensor_copy(pT[:, 8, :], psT[:, j, 0:P]).then_inc(p_kept, 1)
                        dve.tensor_copy(pT[0:NS, 9:12, :].rearrange("p j c -> p (j c)"),
                                        psT[0:NS, j, P:4 * P]).then_inc(p_kept, 1)
                dve.wait_ge(summed, r + 1)
                for pair in range(2):
                    for e in range(2):
                        lane, h = HD * e, 2 * pair + e
                        src = psO[lane:lane + HD, 0:QB * 64].rearrange("p (q c) -> p q c", c=64)[
                            :, :, pair * 32 + h * NEW:pair * 32 + (h + 1) * NEW]
                        at = SEQ + QB * r * NEW
                        dst = oT[lane:lane + HD, pair, at:at + QB * NEW].rearrange("p (q i) -> p q i", i=NEW)
                        dve.tensor_copy(dst, src).then_inc(o_kept, 1)

        @block.scalar
        def _(act):
            for r in range(2):
                act.wait_ge(negated, r + 1)
                if r:
                    act.wait_ge(p_turned, TB * r)
                act.activation(pr[:], S[:], ACT.Exp, bias=nm[:, r:r + 1], scale=SCALE,
                               accum_out=den[:, r:r + 1]).then_inc(expd, 1)


SEGS = ((0, 512), (512, 512), (SEQ, NS))


def conv(nc, io, keep):
    with ExitStack() as ctx:
        n = Names(nc, ctx, "conv")
        NI = CT * 3
        w = n.sb("w", [P, 2, DC, 3, P])
        RS = 2 * NSEQ + 3
        state, stT = n.sb("state", [RS, CW]), n.sb("stT", [P, CT, RS])
        up, us = n.sb("up", [P, 2, 2 + SEQ]), n.sb("us", [P, 2, NSEQ, 2 + NEW])
        cg, y0, y1 = n.sb("cg", [P, 2, 512]), n.sb("y0", [P, 2, 512]), n.sb("y1", [P, 2, 512])
        y2 = n.sb("y2", [P, 2, 512])
        tail, tailT = n.sb("tail", [P, CT, 2 + 2 * NSEQ]), n.sb("tailT", [2 + 2 * NSEQ, CW])
        psZ, psT = n.ps("psZ", [P, 2, 3, 512]), n.ps("psT", [P, 2, 512])
        w_in, small_in = n.sems("w_loaded", 2), n.sem("state_loaded")
        st_turned, st_kept, z_done = n.sem("st_turned"), n.sem("st_kept"), n.sem("z")
        c_kept, padded, u_done = n.sem("c_kept"), n.sem("padded"), n.sem("u")
        y_done, gated, tail_set = n.sem("y"), n.sem("gated"), n.sem("tail_set")
        t_turned, t_kept, stored = n.sem("t_turned"), n.sem("t_kept"), n.sem("stored")
        hT, zT, ident = keep["hT"], keep["zT"], keep["ident"]
        w_v = io["w_in"].rearrange("(c p) n -> p c n", p=P)
        block = ctx.enter_context(nc.Block())

        @block.sync
        def _(sp):
            for j in range(CT):
                if j >= 2:
                    sp.wait_ge(z_done, 3 * (j - 1))
                for s in range(3):
                    at = C_B + s * CW + j * P
                    sp.dma_start(w[:, j % 2, :, s, :], w_v[:, :, at:at + P]).then_inc(w_in[j % 2], 16)
                if j == 0:
                    sp.dma_start(state[0:2 * NSEQ, :], io["state_conv"]).then_inc(small_in, 16)
                    sp.dma_start(state[2 * NSEQ:RS, :], io["conv_w"]).then_inc(small_in, 16)
            sp.wait_ge(t_kept, 2)
            sp.dma_start(io["conv_prompt"], tailT[0:2, :]).then_inc(stored, 16)
            sp.dma_start(io["conv_sample"], tailT[2:2 + 2 * NSEQ, :]).then_inc(stored, 16)
            sp.wait_ge(stored, 32)

        @block.tensor
        def _(pe):
            pe.wait_ge(small_in, 32)
            for j in range(CT):
                last = pe.transpose(psT[:, 0, j * RS:(j + 1) * RS], state[:, j * P:(j + 1) * P],
                                    ident[0:RS, 0:RS])
            last.then_inc(st_turned, 1)
            for i in range(NI):
                j, s = divmod(i, 3)
                a, m = SEGS[s]
                if s == 0:
                    pe.wait_ge(w_in[j % 2], 48 * (j // 2 + 1))
                if i >= 2:
                    pe.wait_ge(gated, i - 1)
                for part in (1, 2, 0):
                    for k in range(DC):
                        last = pe.matmul(psZ[:, i % 2, part, 0:m], w[:, j % 2, k, part, :], hT[:, k, a:a + m],
                                         start=(k == 0), stop=(k == DC - 1))
                last.then_inc(z_done, 1)
            pe.wait_ge(tail_set, 2 * CT)
            NTL = 2 + 2 * NSEQ
            for j in range(CT):
                last = pe.transpose(psT[0:NTL, j // 4, (j % 4) * P:(j % 4 + 1) * P], tail[:, j, :], ident[:])
            last.then_inc(t_turned, 1)

        @block.scalar
        def _(act):
            act.wait_ge(st_turned, 1)
            act.activation(stT[:].rearrange("p j c -> p (j c)"), psT[:, 0, 0:CT * RS], ACT.Copy).then_inc(st_kept, 1)
            for i in range(NI):
                j, s = divmod(i, 3)
                m = SEGS[s][1]
                act.wait_ge(z_done, i + 1)
                if i >= 2:
                    act.wait_ge(u_done, i - 1)
                act.activation(cg[:, i % 2, 0:m], psZ[:, i % 2, 1, 0:m], ACT.Copy).then_inc(c_kept, 1)
            NTL = 2 + 2 * NSEQ
            act.wait_ge(t_turned, 1)
            act.activation(tailT[:, 0:512], psT[0:NTL, 0, :], ACT.Copy).then_inc(t_kept, 1)
            act.activation(tailT[:, 512:CW], psT[0:NTL, 1, 0:CW - 512], ACT.Copy).then_inc(t_kept, 1)

        @block.vector
        def _(dve):
            for s in range(2):
                dve.memset(up[:, s, 0:2], 0.0).then_inc(padded, 1)
            dve.wait_ge(padded, 2)
            dve.wait_ge(st_kept, 1)
            for i in range(NI):
                j, s = divmod(i, 3)
                a, m = SEGS[s]
                if s < 2:
                    U = lambda d: up[:, j % 2, 2 + a - d:2 + a - d + m]
                    shape = lambda ap: ap
                else:
                    U = lambda d: us[:, j % 2, :, 2 - d:2 - d + NEW]
                    shape = lambda ap: ap.rearrange("p (b i) -> p b i", i=NEW)
                    dve.tensor_copy(us[:, j % 2, :, 0:2], stT[:, j, 0:2 * NSEQ].rearrange("p (b k) -> p b k", k=2)
                                    ).then_inc(padded, 1)
                dve.wait_ge(c_kept, i + 1)
                dve.tensor_tensor(U(0), shape(cg[:, i % 2, 0:m]), shape(psZ[:, i % 2, 2, 0:m]),
                                  ALU.mult).then_inc(u_done, 1)
                dve.wait_ge(u_done, i + 1)
                dve.wait_ge(padded, 2 + j + (s == 2))
                if i >= 2:
                    dve.wait_ge(gated, i - 1)
                dve.tensor_scalar(shape(y0[:, i % 2, 0:m]), U(2), stT[:, j, 2 * NSEQ:2 * NSEQ + 1], None,
                                  ALU.mult).then_inc(y_done, 1)
                dve.wait_ge(y_done, 3 * i + 1)
                dve.scalar_tensor_tensor(out=shape(y1[:, i % 2, 0:m]), in0=U(1), scalar=stT[:, j, 2 * NSEQ + 1:2 * NSEQ + 2],
                                         in1=shape(y0[:, i % 2, 0:m]), op0=ALU.mult, op1=ALU.add).then_inc(y_done, 1)
                dve.wait_ge(y_done, 3 * i + 2)
                dve.scalar_tensor_tensor(out=shape(y2[:, i % 2, 0:m]), in0=U(0), scalar=stT[:, j, 2 * NSEQ + 2:2 * NSEQ + 3],
                                         in1=shape(y1[:, i % 2, 0:m]), op0=ALU.mult, op1=ALU.add).then_inc(y_done, 1)
                dve.wait_ge(y_done, 3 * i + 3)
                dve.tensor_tensor(zT[:, j, a:a + m], y2[:, i % 2, 0:m], psZ[:, i % 2, 0, 0:m],
                                  ALU.mult).then_inc(gated, 1)
                if s == 1:
                    dve.tensor_copy(tail[:, j, 0:2], up[:, j % 2, SEQ:SEQ + 2]).then_inc(tail_set, 1)
                if s == 2:
                    dve.tensor_copy(tail[:, j, 2:2 + 2 * NSEQ].rearrange("p (b k) -> p b k", k=2),
                                    us[:, j % 2, :, NEW:NEW + 2]).then_inc(tail_set, 1)


def mix(nc, io, keep):
    with ExitStack() as ctx:
        n = Names(nc, ctx, "mix")
        NI = DC * 3
        KC = (DC, CT, DC, 2)
        AT = (0, DC, DC + CT, 2 * DC + CT)
        w = n.sb("w", [P, 2, sum(KC), P])
        sg, br = n.sb("sg", [P, 2, 2, 512]), n.sb("br", [P, 2, 2, 512])
        psZ = n.ps("psZ", [P, 2, 4, 512])
        w_in = n.sems("w_loaded", 2)
        z_done, gates, weighed, mixed = n.sem("z"), n.sem("gates"), n.sem("weighed"), n.sem("mixed")
        hT, zT, oT, mT = keep["hT"], keep["zT"], keep["oT"], keep["mT"]
        w_v = io["w_in"].rearrange("(c p) n -> p c n", p=P)
        co_v = io["w_conv_o"].rearrange("(c p) n -> p c n", p=P)
        ao_v = io["w_attn_o"].rearrange("(c p) n -> p c n", p=P)
        block = ctx.enter_context(nc.Block())

        @block.sync
        def _(sp):
            for j in range(DC):
                if j >= 2:
                    sp.wait_ge(z_done, 3 * (j - 1))
                for s, (v, col) in enumerate(((w_v, C_GC), (co_v, 0), (w_v, C_GA), (ao_v, 0))):
                    sp.dma_start(w[:, j % 2, AT[s]:AT[s] + KC[s], :],
                                 v[:, :, col + j * P:col + (j + 1) * P]).then_inc(w_in[j % 2], 16)

        @block.tensor
        def _(pe):
            for i in range(NI):
                j, s = divmod(i, 3)
                a, m = SEGS[s]
                if s == 0:
                    pe.wait_ge(w_in[j % 2], 64 * (j // 2 + 1))
                if i >= 2:
                    pe.wait_ge(weighed, 2 * (i - 1))
                for q, src in enumerate((hT, zT, hT, oT)):
                    for k in range(KC[q]):
                        last = pe.matmul(psZ[:, i % 2, q, 0:m], w[:, j % 2, AT[q] + k, :], src[:, k, a:a + m],
                                         start=(k == 0), stop=(k == KC[q] - 1))
                last.then_inc(z_done, 1)

        @block.scalar
        def _(act):
            for i in range(NI):
                m = SEGS[i % 3][1]
                act.wait_ge(z_done, i + 1)
                if i >= 2:
                    act.wait_ge(weighed, 2 * (i - 1))
                for q in range(2):
                    act.activation(sg[:, i % 2, q, 0:m], psZ[:, i % 2, 2 * q, 0:m], ACT.Sigmoid).then_inc(gates, 1)

        @block.vector
        def _(dve):
            for i in range(NI):
                j, s = divmod(i, 3)
                a, m = SEGS[s]
                dve.wait_ge(gates, 2 * (i + 1))
                if i >= 2:
                    dve.wait_ge(mixed, i - 1)
                for q in range(2):
                    dve.tensor_tensor(br[:, i % 2, q, 0:m], sg[:, i % 2, q, 0:m], psZ[:, i % 2, 2 * q + 1, 0:m],
                                      ALU.mult).then_inc(weighed, 1)
                dve.wait_ge(weighed, 2 * (i + 1))
                dve.tensor_tensor(mT[:, j, a:a + m], br[:, i % 2, 0, 0:m], br[:, i % 2, 1, 0:m],
                                  ALU.add).then_inc(mixed, 1)


def out(nc, io, keep):
    with ExitStack() as ctx:
        n = Names(nc, ctx, "out")
        w = n.sb("w", [P, DC, D])
        gate, x, y, x1 = n.sb("gate", [P, 2, D]), n.sb("x", [P, 2, D]), n.sb("y", [P, 2, D]), n.sb("x1", [P, 2, D])
        psM = n.ps("psM", [P, 2, D])
        w_in, x_in, rows_in = n.sems("w_loaded", 2), n.sems("x_loaded", 2), n.sem("rows_loaded")
        projected, gated, added, stored = n.sem("projected"), n.sem("gated"), n.sem("added"), n.sems("stored", 2)
        mT = keep["mT"]
        w_v = io["w_o"].rearrange("(c p) n -> p c n", p=P)
        block = ctx.enter_context(nc.Block())

        @block.sync
        def _(sp):
            for i in range(2):
                sp.dma_start(w[:, :, i * 512:(i + 1) * 512], w_v[:, :, i * 512:(i + 1) * 512]).then_inc(w_in[i], 16)
            for i, t in enumerate((0, PT)):
                load_rows(sp, io, gate[:, i, :], t, 2 * D, rows_in)
            for t in range(NT):
                R = rows_of(t)
                if t >= 2:
                    sp.wait_ge(added, t - 1)
                src = io["x_prompt"][t * P:t * P + R, :] if t < PT else io["x_sample"]
                sp.dma_start(x[0:R, t % 2, :], src).then_inc(x_in[t % 2], 16)

        @block.gpsimd
        def _(pool):
            for t in range(NT):
                R = rows_of(t)
                pool.wait_ge(added, t + 1)
                pool.dma_start(io["x1"][t * P:t * P + R, :], x1[0:R, t % 2, :]).then_inc(stored[t % 2], 16)
            pool.wait_ge(stored[0], 16 * 5)
            pool.wait_ge(stored[1], 16 * 4)

        @block.tensor
        def _(pe):
            for t in range(NT):
                R = rows_of(t)
                if t >= 2:
                    pe.wait_ge(gated, t - 1)
                for i in range(2):
                    if t == 0:
                        pe.wait_ge(w_in[i], 16)
                    for k in range(DC):
                        last = pe.matmul(psM[0:R, t % 2, i * 512:(i + 1) * 512], mT[:, k, t * P:t * P + R],
                                         w[:, k, i * 512:(i + 1) * 512], start=(k == 0), stop=(k == DC - 1))
                last.then_inc(projected, 1)

        @block.vector
        def _(dve):
            dve.wait_ge(rows_in, 32)
            for t in range(NT):
                R = rows_of(t)
                dve.wait_ge(projected, t + 1)
                if t >= 2:
                    dve.wait_ge(added, t - 1)
                dve.tensor_tensor(y[0:R, t % 2, :], psM[0:R, t % 2, :], gate[0:R, t // PT, :],
                                  ALU.mult).then_inc(gated, 1)
                dve.wait_ge(gated, t + 1)
                dve.wait_ge(x_in[t % 2], 16 * (t // 2 + 1))
                if t >= 2:
                    dve.wait_ge(stored[t % 2], 16 * (t // 2))
                dve.tensor_tensor(x1[0:R, t % 2, :], y[0:R, t % 2, :], x[0:R, t % 2, :], ALU.add).then_inc(added, 1)

def wait_apart(eng, sem, value, passed):
    eng.wait_ge(sem, value)
    if not isinstance(value, int):
        eng.sem_inc(passed, 1)


class Link:

    def __init__(self, eng, sem):
        self.eng, self.sem, self.n = eng, sem, 0

    def __call__(self, ins):
        ins.then_inc(self.sem, 1)
        self.n += 1

    def wait(self):
        self.eng.wait_ge(self.sem, self.n)

    def restart(self):
        self.wait()
        self.eng.sem_clear(self.sem)
        self.n = 0


def peer(nc, io, keep):
    with ExitStack() as ctx:
        n = Names(nc, ctx, "peer")
        U, K2 = 8, 2 * KEYS
        V2, HALF = U // 2, TOPK // 2
        LAST = NT * HEADS
        wq, sk, skT = n.sb("wq", [P, DC, HEADS * KD]), n.sb("sk", [P, 2, P]), n.sb("skT", [P, 2, P])
        gain, shift, gate2, gainf = (n.sb(x, [P, D]) for x in ("gain", "shift", "gate2", "gainf"))
        xp, xf, m, h2n, h2 = (n.sb(x, [P, D]) for x in ("xp", "xf", "m", "h2n", "h2"))
        diag = n.sb("diag", [P, HALF, P])
        sq, x2, acc, y = (n.sb(x, [P, D]) for x in ("sq", "x2", "acc", "y"))
        h2T = n.sb("h2T", [P, DC, P])
        small = n.sb("small", [P, 8])
        eps, ss, rt, rs, ssf, rtf, rsf = (small[:, i:i + 1] for i in range(7))
        qn, qT, sc, sc2 = (n.sb(x, [P, K2]) for x in ("qn", "qT", "sc", "sc2"))
        v12, i12 = n.sb("v12", [P, 2, TOPK]), n.sb("i12", [P, 2, TOPK], U32)
        cand, cand2 = n.sb("cand", [P, TOPK, TOPK]), n.sb("cand2", [P, TOPK, TOPK])
        best, pos, ab = n.sb("best", [P, TOPK]), n.sb("pos", [P, TOPK], U32), n.sb("ab", [P, 2, TOPK], U32)
        eq, pick, sel = (n.sb("eq", [P, 2, TOPK, TOPK]), n.sb("pick", [P, 2, TOPK, TOPK]), n.sb("sel", [P, 2, TOPK]))
        iota = n.sb("iota", [P, TOPK])
        nbest, eg, dg, rg = n.sb("nbest", [P, 1]), n.sb("eg", [P, TOPK]), n.sb("dg", [P, 1]), n.sb("rg", [P, 1])
        gates = n.sb("gates", [P, 2, TOPK])
        idx_u, idx_v = n.sb("idx_u", [P, 2, TOPK], U32), n.sb("idx_v", [P, 2, TOPK], U32)
        act_, g1, g2, g3, g4 = (n.sb(x, [P, TOPK]) for x in ("act", "g1", "g2", "g3", "g4"))
        coef = n.sb("coef", [P, 2, TOPK])
        rows_u, rows_v = n.sb("rows_u", [P, U, D]), n.sb("rows_v", [P, 2, V2, D])
        psT = n.ps("psT", [P, DC * P])
        psA = n.ps("psA", [P, D])
        psQ, psQT, psS = n.ps("psQ", [P, 512]), n.ps("psQT", [P, 512]), n.ps("psS", [P, 512])

        const_in, wq_in, row_in, gate_in = n.sem("const_loaded"), n.sem("wq_loaded"), n.sem("rows_loaded"), n.sem("gate_loaded")
        xp_in, xf_in, stored = n.sem("xp_loaded"), n.sem("xf_loaded"), n.sem("stored")
        sk_turned, eps_set = n.sem("sk_turned"), n.sem("eps_set")
        squared, rooted, scaled, shifted = n.sem("squared"), n.sem("rooted"), n.sem("scaled"), n.sem("shifted")
        turned, hT_kept = n.sem("turned"), n.sem("hT_kept")
        q_done, q_kept, qt_done, qt_kept = n.sem("q"), n.sem("q_kept"), n.sem("qt"), n.sem("qt_kept")
        s_done, s_kept = n.sem("s"), n.sem("s_kept")
        pool_passed, pe_passed, dve_passed = n.sem("pool_passed"), n.sem("pe_passed"), n.sem("dve_passed")
        best_neg, gate_exp, gate_used = n.sem("best_neg"), n.sem("gate_exp"), n.sem("gate_used")
        u_named, v_named = n.sem("u_named"), n.sem("v_named")
        u_in, v_in = n.sems("u_in", U), [n.sems("v_even_in", V2), n.sems("v_odd_in", V2)]
        u_free, v_even_free, v_odd_free = n.sem("u_free"), n.sem("v_even_free"), n.sem("v_odd_free")
        coef_set, diag_set, acc_read = n.sem("coef_set"), n.sem("diag_set"), n.sem("acc_read")
        gelu_in, gelu_exp = n.sem("gelu_in"), n.sem("gelu_exp")
        x2_done, f_squared, f_rooted, y_done = n.sem("x2"), n.sem("f_squared"), n.sem("f_rooted"), n.sem("y_done")
        own = n.sem("own")
        ident = keep["ident"]
        block = ctx.enter_context(nc.Block())

        def x1_rows(t, R):
            return io["x1"][bass.ds(t * P, R), :]

        def rows_before(t, kind):
            if isinstance(t, int) and t == 0 and kind == 0:
                return 0
            return NS if isinstance(t, int) and t == PT and kind else P

        def next_rows(t):
            if isinstance(t, int) and t >= PT - 1:
                return NS if t == PT - 1 else 0
            return P

        def rows_of_job(t, kind, ahead):
            if kind + ahead >= HEADS:
                return next_rows(t)
            return rows_of(t) if isinstance(t, int) else P

        def walk(eng, step):
            def tile(t):
                step(t, 0, 0, 0)
                step(t, 1, 1, 1)
                with eng.Fori(1, 3) as p:
                    step(t, 2, 2 * p, 0)
                    step(t, 3, 2 * p + 1, 1)
                step(t, 6, 6, 0)
                step(t, 7, 7, 1)

            tile(0)
            with eng.Fori(1, PT - 1) as t:
                tile(t)
            tile(PT - 1)
            tile(PT)

        @block.sync
        def _(sp):
            def tile(t, R, after=None):
                if after:
                    sp.wait_ge(scaled, t + 1)
                    sp.dma_start(xp[0:after, :], x1_rows(t + 1, after)).then_inc(xp_in, 16)
                if not isinstance(t, int) or t:
                    sp.wait_ge(y_done, t)
                    sp.dma_start(io["y_prompt"][bass.ds((t - 1) * P, P), :], y[:]).then_inc(stored, 16)
                sp.dma_start(xf[0:R, :], x1_rows(t, R)).then_inc(xf_in, 16)

            sp.dma_start(xp[:], x1_rows(0, P)).then_inc(xp_in, 16)
            load_rows(sp, io, gain, 0, 4 * D, row_in)
            load_rows(sp, io, shift, 0, 3 * D, row_in)
            sp.dma_start(sk[:], io["sub_keys"].rearrange("s k d -> k s d")).then_inc(const_in, 16)
            sp.dma_start(iota[:], io["iota16"]).then_inc(const_in, 16)
            wq_v = io["w_query"].rearrange("(c p) n -> p c n", p=P)
            sp.dma_start(wq[:, :, 0:D], wq_v[:, :, 0:D]).then_inc(wq_in, 16)
            sp.dma_start(wq[:, :, D:2 * D], wq_v[:, :, D:2 * D]).then_inc(wq_in, 16)
            load_rows(sp, io, gate2, 0, 5 * D, gate_in)
            sp.dma_start(gainf[:], io["norm_f_g"].broadcast_to([P, D])).then_inc(gate_in, 16)
            tile(0, P, P)
            with sp.Fori(1, PT - 1) as t:
                tile(t, P, P)
            sp.wait_ge(shifted, PT)
            load_rows(sp, io, gain, PT, 4 * D, row_in)
            load_rows(sp, io, shift, PT, 3 * D, row_in)
            tile(PT - 1, P, NS)
            sp.wait_ge(y_done, PT)
            load_rows(sp, io, gate2, PT, 5 * D, gate_in)
            tile(PT, NS)
            sp.wait_ge(y_done, NT)
            sp.dma_start(io["y_sample"], y[0:NS, :]).then_inc(stored, 16)
            sp.wait_ge(stored, 16 * NT)

        @block.gpsimd
        def _(pool):
            pool.memset(eps, EPS).then_inc(eps_set, 1)
            passed = pool_passed

            def gather(table, idx, k, R, dst, landed):
                pool.indirect_dma_start(
                    out=dst, out_offset=None, in_=table,
                    in_offset=bass.IndirectOffsetOnAxis(ap=idx[0:R, k:k + 1], axis=0)).then_inc(landed, 16)

            def step(s, b, RU, RV):
                for i in range(TOPK // 4):
                    if RU:
                        if i == 0:
                            wait_apart(pool, u_named, s + 1, passed)
                        wait_apart(pool, u_free, TOPK * s + 4 * i + 4, passed)
                        for k in range(4 * i, 4 * i + 4):
                            gather(io["expert_u"], idx_u[:, b], k, RU, rows_u[0:RU, k % U, :], u_in[k % U])
                    if RV:
                        if i == 0:
                            wait_apart(pool, v_named, s, passed)
                        wait_apart(pool, v_even_free, HALF * (s - 1) + 2 * i + 2, passed)
                        wait_apart(pool, v_odd_free, HALF * (s - 1) + 2 * i + 2, passed)
                        for k in range(4 * i, 4 * i + 4):
                            gather(io["expert_v"], idx_v[:, 1 - b], k, RV,
                                   rows_v[0:RV, k % 2, k // 2 % V2, :], v_in[k % 2][k // 2 % V2])

            S0 = PT * HEADS
            step(0, 0, P, 0)
            step(1, 1, P, P)
            with pool.Fori(1, S0 // 2) as q:
                step(2 * q, 0, P, P)
                step(2 * q + 1, 1, P, P)
            step(S0, 0, NS, P)
            step(S0 + 1, 1, NS, NS)
            with pool.Fori(S0 // 2 + 1, LAST // 2) as q:
                step(2 * q, 0, NS, NS)
                step(2 * q + 1, 1, NS, NS)
            step(LAST, 0, 0, NS)

        @block.tensor
        def _(pe):
            def wait(sem, value):
                wait_apart(pe, sem, value, pe_passed)

            def turn(t, R):
                wait(shifted, t + 1)
                for k in range(DC):
                    last = pe.transpose(psT[:, k * P:k * P + R], h2n[0:R, k * P:(k + 1) * P], ident[0:R, 0:R])
                last.then_inc(turned, 1)

            def query(j, h, R):
                wait(s_kept, j + 1)
                for k in range(DC):
                    last = pe.matmul(psQ[0:R, 0:KD], h2T[:, k, 0:R], wq[:, k, bass.ds(h * KD, KD)],
                                     start=(k == 0), stop=(k == DC - 1))
                last.then_inc(q_done, 1)
                wait(q_kept, j + 1)
                for i in range(2):
                    last = pe.transpose(psQT[:, i * P:i * P + R], qn[0:R, i * P:(i + 1) * P], ident[0:R, 0:R])
                last.then_inc(qt_done, 1)
                wait(qt_kept, j + 1)
                for i in range(2):
                    last = pe.matmul(psS[0:R, i * KEYS:(i + 1) * KEYS], qT[:, i * P:i * P + R], skT[:, i, :],
                                     start=True, stop=True)
                last.then_inc(s_done, 1)

            pe.wait_ge(const_in, 32)
            for i in range(2):
                last = pe.transpose(psQ[:, i * P:(i + 1) * P], sk[:, i, :], ident[:])
            last.then_inc(sk_turned, 1)
            pe.wait_ge(wq_in, 32)

            def add_row(s, i, R, first):
                wait(diag_set, HALF * s + i + 1)
                wait(v_in[1][i % V2], 16 * (2 * s + i // V2 + 1))
                for c in range(2):
                    last = pe.matmul(psA[0:R, c * 512:(c + 1) * 512], diag[0:R, i, 0:R],
                                     rows_v[0:R, 1, i % V2, c * 512:(c + 1) * 512],
                                     start=(first and i == 0), stop=False, skip_group_check=True)
                last.then_inc(v_odd_free, 1)

            def step(t, kind, h, b):
                s = t * HEADS + h
                RV = rows_before(t, kind)
                first = kind == 1
                if first and not (isinstance(t, int) and t == 0):
                    wait(acc_read, t)
                for i in range(HALF // 2):
                    if RV:
                        add_row(s - 1, i, RV, first)
                if kind == 6 and next_rows(t):
                    turn(t + 1, next_rows(t))
                    wait(hT_kept, 2 * (t + 2))
                R = rows_of_job(t, kind, 2)
                if R:
                    query(s + 2, h + 2 if kind < 6 else kind - 6, R)
                for i in range(HALF // 2, HALF):
                    if RV:
                        add_row(s - 1, i, RV, first)

            turn(0, P)
            pe.wait_ge(hT_kept, 2)
            query(0, 0, P)
            query(1, 1, P)
            walk(pe, step)
            for i in range(HALF):
                add_row(LAST - 1, i, NS, False)

        @block.scalar
        def _(act):
            def prep(t, R):
                act.wait_ge(xp_in, 16 * (t + 1))
                act.activation(sq[0:R, :], xp[0:R, :], ACT.Square, accum_out=ss[0:R, :]).then_inc(squared, 1)
                act.wait_ge(squared, t + 1)
                act.activation(rt[0:R, :], ss[0:R, :], ACT.Sqrt, bias=eps[0:R, :], scale=1.0 / D).then_inc(rooted, 1)
                act.wait_ge(turned, t + 1)
                for i in range(2):
                    src = psT[:, i * 512:(i + 1) * 512].rearrange("p (c r) -> p c r", r=P)[:, :, 0:R]
                    act.activation(h2T[:, 4 * i:4 * i + 4, 0:R], src, ACT.Copy).then_inc(hT_kept, 1)

            def scores(j, R):
                act.wait_ge(q_done, j + 1)
                act.activation(qn[0:R, :], psQ[0:R, 0:KD], ACT.Copy).then_inc(q_kept, 1)
                act.wait_ge(qt_done, j + 1)
                src = psQT[:, 0:2 * P].rearrange("p (i r) -> p i r", r=P)[:, :, 0:R]
                act.activation(qT[:].rearrange("p (i r) -> p i r", r=P)[:, :, 0:R], src, ACT.Copy).then_inc(qt_kept, 1)
                act.wait_ge(s_done, j + 1)
                if not isinstance(j, int) or j:
                    act.wait_ge(best_neg, j)
                act.activation(sc[0:R, :], psS[0:R, 0:K2], ACT.Copy).then_inc(s_kept, 1)

            def gate(j, R):
                act.wait_ge(best_neg, j + 1)
                if not isinstance(j, int) or j:
                    act.wait_ge(gate_used, j)
                act.activation(eg[0:R, :], best[0:R, :], ACT.Exp, bias=nbest[0:R, :],
                               accum_out=dg[0:R, :]).then_inc(gate_exp, 1)

            def final(t, R):
                act.wait_ge(x2_done, t + 1)
                act.activation(sq[0:R, :], x2[0:R, :], ACT.Square, accum_out=ssf[0:R, :]).then_inc(f_squared, 1)
                act.wait_ge(f_squared, t + 1)
                act.activation(rtf[0:R, :], ssf[0:R, :], ACT.Sqrt, bias=eps[0:R, :],
                               scale=1.0 / D).then_inc(f_rooted, 1)

            def spread(s, b, R):
                act.wait_ge(coef_set, s + 1)
                for i in range(HALF):
                    if i == 0 and not (isinstance(s, int) and s == 0):
                        act.wait_ge(v_odd_free, V2 + HALF * s)
                    act.activation(diag[0:R, i, 0:R], ident[0:R, 0:R], ACT.Copy,
                                   scale=coef[0:R, b, 2 * i + 1:2 * i + 2]).then_inc(diag_set, 1)

            def step(t, kind, h, b):
                s = t * HEADS + h
                R = rows_of(t) if isinstance(t, int) else P
                RV, R1, R2 = rows_before(t, kind), rows_of_job(t, kind, 1), rows_of_job(t, kind, 2)
                if RV:
                    spread(s - 1, 1 - b, RV)
                if R1:
                    gate(s + 1, R1)
                if kind == 6 and next_rows(t):
                    prep(t + 1, next_rows(t))
                if R2:
                    scores(s + 2, R2)
                act.wait_ge(gelu_in, s + 1)
                act.activation(g4[0:R, :], g3[0:R, :], ACT.Exp, scale=-GELU).then_inc(gelu_exp, 1)
                if kind == 0 and not (isinstance(t, int) and t == 0):
                    final(t - 1, P)

            act.wait_ge(eps_set, 1)
            act.wait_ge(sk_turned, 1)
            act.activation(skT[:].rearrange("p i k -> p (i k)"), psQ[:, 0:2 * P], ACT.Copy).then_inc(s_kept, 1)
            prep(0, P)
            scores(0, P)
            gate(0, P)
            scores(1, P)
            walk(act, step)
            spread(LAST - 1, 1, NS)
            final(PT, NS)

        @block.vector
        def _(dve):
            link = Link(dve, own)

            def prep(t, R):
                dve.wait_ge(row_in, 32 if R == P else 64)
                dve.wait_ge(rooted, t + 1)
                link(dve.reciprocal(rs[0:R, :], rt[0:R, :]))
                link.wait()
                dve.scalar_tensor_tensor(out=m[0:R, :], in0=xp[0:R, :], scalar=rs[0:R, :], in1=gain[0:R, :],
                                         op0=ALU.mult, op1=ALU.mult).then_inc(scaled, 1)
                dve.wait_ge(scaled, t + 1)
                dve.tensor_tensor(h2n[0:R, :], m[0:R, :], shift[0:R, :], ALU.add).then_inc(shifted, 1)

            def experts(j, b, R):
                def halves(f):
                    for i in range(2):
                        f(i, sc[0:R, i * KEYS:(i + 1) * KEYS], sc2[0:R, i * KEYS:(i + 1) * KEYS])
                    link.wait()

                wait_apart(dve, s_kept, j + 2, dve_passed)
                halves(lambda i, a, b: link(dve.max(v12[0:R, i, 0:8], a)))

                def second(i, a, b):
                    link(dve.max_index(i12[0:R, i, 0:8], v12[0:R, i, 0:8], a))
                    link(dve.match_replace(b, v12[0:R, i, 0:8], a, LOW))

                halves(second)
                halves(lambda i, a, b: link(dve.max(v12[0:R, i, 8:16], b)))
                halves(lambda i, a, b: link(dve.max_index(i12[0:R, i, 8:16], v12[0:R, i, 8:16], b)))
                c, c2 = (x[0:R].rearrange("p a b -> p (a b)") for x in (cand, cand2))
                link(dve.tensor_tensor(cand[0:R], v12[0:R, 0, :].unsqueeze(2).broadcast_to([R, TOPK, TOPK]),
                                       v12[0:R, 1:2, :].broadcast_to([R, TOPK, TOPK]), ALU.add))
                link.wait()
                link(dve.max(best[0:R, 0:8], c))
                link.wait()
                link(dve.max_index(pos[0:R, 0:8], best[0:R, 0:8], c))
                link(dve.match_replace(c2, best[0:R, 0:8], c, LOW))
                link.wait()
                link(dve.max(best[0:R, 8:16], c2))
                link.wait()
                dve.tensor_scalar(nbest[0:R, :], best[0:R, 0:1], -1.0, None, ALU.mult).then_inc(best_neg, 1)
                link(dve.max_index(pos[0:R, 8:16], best[0:R, 8:16], c2))
                link.wait()
                link(dve.tensor_scalar(ab[0:R, 0, :], pos[0:R, :], 4, None, ALU.logical_shift_right))
                link(dve.tensor_scalar(ab[0:R, 1, :], pos[0:R, :], 15, None, ALU.bitwise_and))
                link.wait()
                shape = [R, 2, TOPK, TOPK]
                link(dve.tensor_tensor(eq[0:R], ab[0:R].unsqueeze(3).broadcast_to(shape),
                                       iota[0:R].unsqueeze(1).unsqueeze(1).broadcast_to(shape), ALU.is_equal))
                link.wait()
                link(dve.tensor_tensor(pick[0:R], eq[0:R], i12[0:R].unsqueeze(2).broadcast_to(shape), ALU.mult))
                link.wait()
                link(dve.tensor_reduce(sel[0:R], pick[0:R], AX, ALU.add))
                link.wait()
                dve.scalar_tensor_tensor(out=idx_u[0:R, b, :], in0=sel[0:R, 0, :], scalar=float(KEYS),
                                         in1=sel[0:R, 1, :], op0=ALU.mult, op1=ALU.add).then_inc(u_named, 1)
                dve.wait_ge(gate_exp, j + 1)
                link(dve.reciprocal(rg[0:R, :], dg[0:R, :]))
                link.wait()
                dve.tensor_scalar(gates[0:R, b, :], eg[0:R, :], rg[0:R, :], None,
                                  ALU.mult).then_inc(gate_used, 1)

            def final(t, R):
                dve.wait_ge(v_even_free, V2 + HALF * HEADS * (t + 1))
                dve.wait_ge(v_odd_free, V2 + HALF * HEADS * (t + 1))
                dve.tensor_tensor(acc[0:R, :], acc[0:R, :], psA[0:R, :], ALU.add).then_inc(acc_read, 1)
                dve.wait_ge(acc_read, t + 1)
                dve.wait_ge(gate_in, 32 if R == P else 48)
                link(dve.tensor_tensor(m[0:R, :], acc[0:R, :], gate2[0:R, :], ALU.mult))
                link.wait()
                dve.wait_ge(xf_in, 16 * (t + 1))
                dve.tensor_tensor(x2[0:R, :], m[0:R, :], xf[0:R, :], ALU.add).then_inc(x2_done, 1)
                dve.wait_ge(f_rooted, t + 1)
                link(dve.reciprocal(rsf[0:R, :], rtf[0:R, :]))
                link.wait()
                if not isinstance(t, int) or t:
                    dve.wait_ge(stored, 16 * t)
                dve.scalar_tensor_tensor(out=y[0:R, :], in0=x2[0:R, :], scalar=rsf[0:R, :], in1=gainf[0:R, :],
                                         op0=ALU.mult, op1=ALU.mult).then_inc(y_done, 1)

            def dot(s, k, R):
                dve.wait_ge(u_in[k % U], 16 * (2 * s + k // U + 1))
                dve.tensor_tensor_reduce(rows_u[0:R, k % U, :], rows_u[0:R, k % U, :], h2[0:R, :], 1.0, 0.0, ALU.mult, ALU.add,
                                         act_[0:R, k:k + 1]).then_inc(u_free, 1)

            def add_row(s, i, R, b, first):
                if i == 0:
                    dve.wait_ge(coef_set, s + 1)
                dve.wait_ge(v_in[0][i % V2], 16 * (2 * s + i // V2 + 1))
                c = coef[0:R, b, 2 * i:2 * i + 1]
                if first:
                    dve.tensor_scalar(acc[0:R, :], rows_v[0:R, 0, i % V2, :], c, None,
                                      ALU.mult).then_inc(v_even_free, 1)
                    return
                dve.wait_ge(v_even_free, V2 + HALF * s + i)
                dve.scalar_tensor_tensor(out=acc[0:R, :], in0=rows_v[0:R, 0, i % V2, :], scalar=c,
                                         in1=acc[0:R, :], op0=ALU.mult, op1=ALU.add).then_inc(v_even_free, 1)

            def coefs(s, R, b):
                a = act_[0:R, :]
                dve.wait_ge(u_free, U + TOPK * (s + 1))
                link(dve.tensor_tensor(g1[0:R, :], a, a, ALU.mult))
                link.wait()
                link(dve.tensor_scalar(g2[0:R, :], g1[0:R, :], 0.044715, 1.0, ALU.mult, ALU.add))
                link.wait()
                link(dve.tensor_tensor(g1[0:R, :], g2[0:R, :], a, ALU.mult))
                link.wait()
                dve.tensor_scalar(g3[0:R, :], g1[0:R, :], -50.0, None, ALU.max).then_inc(gelu_in, 1)
                dve.wait_ge(gelu_exp, s + 1)
                link(dve.tensor_scalar(g1[0:R, :], g4[0:R, :], 1.0, None, ALU.add))
                link.wait()
                link(dve.reciprocal(g2[0:R, :], g1[0:R, :]))
                link.wait()
                link(dve.tensor_tensor(g1[0:R, :], g2[0:R, :], a, ALU.mult))
                link.wait()
                if not isinstance(s, int) or s >= 2:
                    dve.wait_ge(diag_set, HALF * (s - 1))
                dve.tensor_tensor(coef[0:R, b, :], g1[0:R, :], gates[0:R, b, :], ALU.mult).then_inc(coef_set, 1)

            def step(t, kind, h, b):
                s = t * HEADS + h
                at = isinstance(t, int)
                R = rows_of(t) if at else P
                RV, R1 = rows_before(t, kind), rows_of_job(t, kind, 1)
                if kind == 0:
                    dve.wait_ge(u_free, U + TOPK * s)
                    dve.wait_ge(shifted, t + 1)
                    link(dve.tensor_copy(h2[0:R, :], h2n[0:R, :]))
                link.restart()
                if R1:
                    experts(s + 1, 1 - b, R1)
                dve.wait_ge(u_named, s + 1)
                if not isinstance(s, int) or s >= 2:
                    dve.wait_ge(v_odd_free, V2 + HALF * (s - 1))
                dve.tensor_copy(idx_v[0:R, b, :], idx_u[0:R, b, :]).then_inc(v_named, 1)
                if kind == 6 and next_rows(t):
                    prep(t + 1, next_rows(t))
                for k in range(TOPK):
                    dot(s, k, R)
                    if RV and k % 2 == 0:
                        add_row(s - 1, k // 2, RV, 1 - b, kind == 1 and k == 0)
                coefs(s, R, b)
                if kind == 0 and not (at and t == 0):
                    final(t - 1, P)

            dve.memset(coef[:], 0.0).then_inc(u_free, U)
            dve.memset(act_[:], 0.0).then_inc(v_even_free, V2)
            dve.memset(g4[:], 0.0).then_inc(v_odd_free, V2)
            dve.wait_ge(const_in, 32)
            prep(0, P)
            experts(0, 0, P)
            walk(dve, step)
            for i in range(HALF):
                add_row(LAST - 1, i, NS, 1, False)
            final(PT, NS)


def layer(nc, io):
    with ExitStack() as whole:
        top = Names(nc, whole, "keep")
        keep = {"ident": top.sb("ident", [P, P])}
        ada(nc, io, keep)
        with ExitStack() as front:
            f = Names(nc, front, "front")
            keep["hT"] = f.sb("hT", [P, DC, TOK])
            keep["oT"] = f.sb("oT", [P, 2, TOK])
            norm(nc, io, keep)
            with ExitStack() as heads:
                s = Names(nc, heads, "smp")
                keep["qTs"], keep["kTs"] = s.sb("qTs", [P, 6, NS]), s.sb("kTs", [P, 6, NS])
                keep["Vs"] = s.sb("Vs", [NS, AW])
                with ExitStack() as prompt:
                    p = Names(nc, prompt, "prompt")
                    keep["qT"], keep["kT"] = p.sb("qT", [P, 6, SEQ]), p.sb("kT", [P, 6, SEQ])
                    keep["V"] = p.sb("V", [P, PT, AW])
                    qkv(nc, io, keep)
                    attend(nc, io, keep)
                sampled(nc, io, keep)
            with ExitStack() as branches:
                b = Names(nc, branches, "branches")
                keep["mT"] = b.sb("mT", [P, DC, TOK])
                with ExitStack() as z:
                    keep["zT"] = Names(nc, z, "z").sb("zT", [P, CT, TOK])
                    conv(nc, io, keep)
                    mix(nc, io, keep)
                out(nc, io, keep)
        peer(nc, io, keep)


def kernel(x_prompt, x_sample, cache_kv0, cache_kv1, cache_kv2, state_conv, c_prompt, c_sample, norm1_g, norm2_g,
           norm_f_g, w_ada, b_ada, w_in, conv_w, w_attn_o, w_conv_o, w_o, w_query, sub_keys, expert_u, expert_v):
    import concourse.bacc as bacc
    from concourse.bass_utils import run_bass_kernel_spmd

    a = {
        "x_prompt": x_prompt[0], "x_sample": x_sample.reshape(NS, D), "state_conv": state_conv.reshape(2 * NSEQ, CW),
        "c_prompt": c_prompt, "c_sample": c_sample, "norm1_g": norm1_g, "norm2_g": norm2_g,
        "norm_f_g": norm_f_g.reshape(1, D), "w_ada": w_ada[0], "b_ada": b_ada, "w_in": w_in[0], "conv_w": conv_w[0],
        "w_attn_o": w_attn_o[0], "w_conv_o": w_conv_o[0], "w_o": w_o[0], "w_query": w_query[0],
        "sub_keys": sub_keys[0], "expert_u": expert_u[0], "expert_v": expert_v[0],
    }
    for g, c in enumerate((cache_kv0, cache_kv1, cache_kv2)):
        a[f"cache{g}"] = c[0].reshape(NSEQ, CACHE[g], 2, SLOTS * HD)
    a.update(constants())
    a = {k: np.ascontiguousarray(v) for k, v in a.items()}
    nc = bacc.Bacc("TRN2", target_bir_lowering=False, num_devices=1)
    io = {k: nc.dram_tensor(f"in_{k}", v.shape, F32, kind="ExternalInput").ap() for k, v in a.items()}
    io["cache"] = [io[f"cache{g}"] for g in range(GROUPS)]
    outs = []

    def output(shape):
        outs.append(f"out_{len(outs)}")
        return nc.dram_tensor(outs[-1], shape, F32, kind="ExternalOutput").ap()

    io["y_prompt"], io["y_sample"] = output((SEQ, D)), output((NS, D))
    io["kvp"] = [output((min(w, SEQ), 2, SLOTS * HD)) for w in WINDOWS]
    io["conv_prompt"] = output((2, CW))
    io["kvs"] = [output((NS, 2, SLOTS * HD)) for _ in WINDOWS]
    io["conv_sample"] = output((2 * NSEQ, CW))
    io["mod"] = nc.dram_tensor("mod_rows", (1 + NSEQ, 6 * D), F32, kind="Internal").ap()
    io["x1"] = nc.dram_tensor("x_after_mixing", (TOK, D), F32, kind="Internal").ap()
    layer(nc, io)
    got = run_bass_kernel_spmd(nc, [{f"in_{k}": v for k, v in a.items()}], core_ids=[0]).results[0]
    shapes = ([(1, SEQ, D), (NSEQ, NEW, D)] + [(1, 1, min(w, SEQ), 2, SLOTS, HD) for w in WINDOWS] + [(1, 1, 2, CW)]
              + [(1, NSEQ, NEW, 2, SLOTS, HD)] * GROUPS + [(1, NSEQ, 2, CW)])
    return tuple(got[n].reshape(s) for n, s in zip(outs, shapes))
```

```python
from contextlib import ExitStack

import concourse.bass as bass
import numpy as np
from concourse import mybir

F32 = mybir.dt.float32
BF16 = mybir.dt.bfloat16
U32 = mybir.dt.uint32
ALU = mybir.AluOpType
ACT = mybir.ActivationFunctionType
AX = mybir.AxisListType.X

P = 128
D = 1024
DC = D // P
SEQ = 1024
NSEQ = 8
NEW = 8
NS = NSEQ * NEW
TOK = SEQ + NS
PT = SEQ // P
NT = PT + 1
PAST = 1024
HD = 64
WINDOWS = (128, 512, 2048)
DILS = (1, 4, 16)
CACHE = tuple(min(w, PAST) for w in WINDOWS)
GROUPS = 3
SLOTS = 4
AW = GROUPS * SLOTS * HD
CW = 768
CT = CW // P
EPS = 1e-6
SCALE = HD ** -0.5
MASKED = -1e30
C_Q, C_K, C_V, C_B = 0, AW, 2 * AW, 3 * AW
C_GA = 3 * AW + 3 * CW
C_GC = C_GA + D
HEADS = 8
KEYS = 128
TOPK = 16
KD = 256
GELU = 2 * (2 / np.pi) ** 0.5
LOW = -3e38


def rows_of(t):
    return P if t < PT else NS


def constants():
    half = HD // 2
    inv = (10000.0 ** (-np.arange(half, dtype=np.float32) / half)).astype(np.float32)
    pos = np.concatenate([np.arange(SEQ), np.tile(PAST + np.arange(NEW), NSEQ)]).astype(np.float32)
    ang = (pos[:, None] * inv[None, :]).astype(np.float32)
    c, s = np.cos(ang), np.sin(ang)
    rope = np.concatenate([c, c, -s, s], axis=1).astype(np.float32)
    rope = np.concatenate([rope, np.zeros((NT * P - TOK, 4 * half), np.float32)])
    q = np.arange(P)[:, None, None]
    key = np.arange(P)[None, None, :]
    parts = []
    for g in (2, 1, 0):
        n = BLOCKS[g]
        back = (n - 1 - np.arange(n))[None, :, None]
        dist = back * P + q - key
        ok = (dist >= 0) & (dist <= WINDOWS[g]) & (dist % DILS[g] == 0)
        parts.append(np.where(ok, 0.0, MASKED).reshape(P, n * P))
    pmask = np.concatenate(parts, axis=1).astype(np.float32)
    row = np.arange(P)
    i = (row % NEW)[:, None]
    p = np.arange(P)[None, :]
    smask = np.zeros((2, P, SCOLS), np.float32)
    for j in range(4):
        d1 = i + CACHE[1] - (4 * p + j)
        smask[:, :, j * P:(j + 1) * P] = np.where((d1 <= WINDOWS[1]) & (d1 % DILS[1] == 0), 0.0, MASKED)
        d2 = i + CACHE[2] - (16 * (p % 64) + 4 * (p // 64) + j)
        smask[:, :, (4 + j) * P:(5 + j) * P] = np.where((d2 <= WINDOWS[2]) & (d2 % DILS[2] == 0), 0.0, MASKED)
    d0 = i + CACHE[0] - p
    smask[:, :, 8 * P:9 * P] = np.where(d0 <= WINDOWS[0], 0.0, MASKED)
    b2, i2 = np.arange(NS)[None, :] // NEW, np.arange(NS)[None, :] % NEW
    for r in range(2):
        b = (4 * r + row // 32)[:, None]
        for g in range(GROUPS):
            ok = (b2 == b) & (i2 <= i) & ((i - i2) % DILS[g] == 0)
            smask[r, :, SNEW + g * NS:SNEW + (g + 1) * NS] = np.where(ok, 0.0, MASKED)
    return {
        "rope": rope, "pmask": pmask, "smask": smask, "ident": np.eye(P, dtype=np.float32),
        "iota16": np.tile(np.arange(TOPK, dtype=np.float32), (P, 1)),
    }


BLOCKS = tuple(min(w // P, PT - 1) + 1 for w in WINDOWS)
SBLK = 9
SNEW = SBLK * P
SCOLS = SNEW + GROUPS * NS


def key_blocks(t):
    return [(g, kb) for g in (2, 1, 0) for kb in range(max(0, t - BLOCKS[g] + 1), t + 1)]


NMASK = sum(BLOCKS)
WQKV = 384
QKV_AHEAD = 1
MASK_AT = {2: 0, 1: BLOCKS[2], 0: BLOCKS[2] + BLOCKS[1]}


def mask_block(g, t, kb):
    return MASK_AT[g] + BLOCKS[g] - 1 - (t - kb)


class Names:

    spent = []

    def __init__(self, nc, ctx, name):
        self.nc, self.ctx, self.name = nc, ctx, name

    @classmethod
    def recycle(cls, nc):
        nc.clear_and_free_semaphores(cls.spent)
        nc.all_engine_barrier()
        cls.spent = []

    def sb(self, name, shape, dt=F32):
        return self.ctx.enter_context(self.nc.sbuf_tensor(f"{self.name}_{name}", shape, dt))

    def ps(self, name, shape, dt=F32):
        return self.ctx.enter_context(self.nc.psum_tensor(f"{self.name}_{name}", shape, dt))

    def sem(self, name):
        self.spent.append(self.nc.alloc_semaphore(f"{self.name}_{name}"))
        return self.spent[-1]

    def sems(self, name, n):
        return [self.sem(f"{name}{i}") for i in range(n)]


def rep_rows(src, row0, rows, reps, stride, col, n):
    return bass.AP(src.tensor, src.offset + row0 * stride + col, [[stride, rows], [0, reps], [1, n]])


ADA_W = 512
ADA_GROUPS = 6 * D // ADA_W
ADA_FIRST = 2 * D // ADA_W
NQ = 1 + NSEQ


def load_ada(eng, io, keep, g, sem):
    w_v = io["w_ada"].rearrange("(c p) n -> p c n", p=P)
    eng.dma_start(keep["w_ada"][:, g % 2], w_v[:, :, g * ADA_W:(g + 1) * ADA_W]).then_inc(sem, 16)


def project_ada(pe, keep, dst, g):
    for k in range(DC):
        last = pe.matmul(dst, keep["cT"][:, k, :], keep["w_ada"][:, g % 2, k, :], start=(k == 0), stop=(k == DC - 1))
    return last


def ada(nc, io, keep):
    with ExitStack() as ctx:
        n = Names(nc, ctx, "ada")
        W, NG = ADA_W, ADA_FIRST
        c, e, sc = n.sb("c", [NQ, D]), n.sb("e", [NQ, D]), n.sb("silu", [NQ, D])
        cT, mod, gains = keep["cT"], keep["mod"], keep["gains"]
        psT, psM = n.ps("psT", [P, 512]), n.ps("psM", [P, 2, 512])
        loaded, consts = n.sem("c_loaded"), n.sem("rows_loaded")
        w_in, ahead = n.sems("w_loaded", 2), n.sem("loaded_ahead")
        exp_done, silu_done, tr_done, cT_done = n.sem("exp"), n.sem("silu_s"), n.sem("tr"), n.sem("cT_s")
        mm_done, added, scaled, stored = n.sem("mm"), n.sem("added"), n.sem("scaled"), n.sem("stored")
        block = ctx.enter_context(nc.Block())

        @block.sync
        def _(sp):
            sp.dma_start(c[0:1, :], io["c_prompt"]).then_inc(loaded, 16)
            sp.dma_start(c[1:NQ, :], io["c_sample"]).then_inc(loaded, 16)
            sp.dma_start(keep["ident"][:], io["ident"]).then_inc(loaded, 16)
            for g in range(NG):
                if g >= 2:
                    sp.wait_ge(mm_done, g - 1)
                load_ada(sp, io, keep, g, w_in[g % 2])
                if g == 0:
                    sp.dma_start(mod[:], io["b_ada"].broadcast_to([NQ, 6 * D])).then_inc(consts, 16)
                    sp.dma_start(gains[:, 0, :], io["norm1_g"].broadcast_to([NQ, D])).then_inc(consts, 16)
                    sp.dma_start(gains[:, 1, :], io["norm2_g"].broadcast_to([NQ, D])).then_inc(consts, 16)
            sp.wait_ge(mm_done, NG - 1)
            load_ada(sp, io, keep, NG, ahead)
            sp.wait_ge(scaled, 1)
            sp.dma_start(io["mod"][:, 0:2 * D], mod[:, 0:2 * D]).then_inc(stored, 16)
            sp.wait_ge(stored, 16)
            sp.wait_ge(ahead, 16)

        @block.scalar
        def _(act):
            act.wait_ge(loaded, 48)
            act.activation(e[:], c[:], ACT.Exp, scale=-1.0).then_inc(exp_done, 1)

        @block.tensor
        def _(pe):
            pe.wait_ge(silu_done, 3)
            for k in range(DC):
                last = pe.transpose(psT[:, k * NQ:(k + 1) * NQ], sc[:, k * P:(k + 1) * P],
                                    keep["ident"][0:NQ, 0:NQ])
            last.then_inc(tr_done, 1)
            pe.wait_ge(cT_done, 1)
            for g in range(NG):
                pe.wait_ge(w_in[g % 2], 16 * (g // 2 + 1))
                if g >= 2:
                    pe.wait_ge(added, g - 1)
                project_ada(pe, keep, psM[0:NQ, g % 2, :], g).then_inc(mm_done, 1)

        @block.vector
        def _(dve):
            dve.wait_ge(exp_done, 1)
            dve.tensor_scalar(e[:], e[:], 1.0, None, ALU.add).then_inc(silu_done, 1)
            dve.wait_ge(silu_done, 1)
            dve.reciprocal(sc[:], e[:]).then_inc(silu_done, 1)
            dve.wait_ge(silu_done, 2)
            dve.tensor_tensor(sc[:], sc[:], c[:], ALU.mult).then_inc(silu_done, 1)
            dve.wait_ge(tr_done, 1)
            dve.tensor_copy(cT[:].rearrange("p c n -> p (c n)"), psT[:, 0:DC * NQ]).then_inc(cT_done, 1)
            dve.wait_ge(consts, 48)
            for g in range(NG):
                dve.wait_ge(mm_done, g + 1)
                dve.tensor_tensor(mod[:, g * W:(g + 1) * W], psM[0:NQ, g % 2, :], mod[:, g * W:(g + 1) * W],
                                  ALU.add).then_inc(added, 1)
            dve.wait_ge(added, NG)
            dve.scalar_tensor_tensor(out=mod[:, D:2 * D], in0=mod[:, D:2 * D], scalar=1.0, in1=gains[:, 0, :],
                                     op0=ALU.add, op1=ALU.mult).then_inc(scaled, 1)


def load_rows(eng, io, dst, t, col, sem):
    if t < PT:
        src = rep_rows(io["mod"], 0, 1, P, 6 * D, col, D)
    else:
        src = rep_rows(io["mod"], 1, NSEQ, NEW, 6 * D, col, D)
    return eng.dma_start(dst[0:rows_of(t), :], src).then_inc(sem, 16)


def load_qkv(eng, io, keep, g, sem):
    w_v = io["w_in"].rearrange("(c p) n -> p c n", p=P)
    slots = keep["w_qkv"]
    dst = slots[g % len(slots)].rearrange("p (c n) -> p c n", c=DC)
    eng.dma_start(dst, w_v[:, :, g * WQKV:(g + 1) * WQKV]).then_inc(sem, 16)


def load_conv(eng, io, keep, j, sem):
    w_v = io["w_in"].rearrange("(c p) n -> p c n", p=P)
    for s in range(3):
        at = C_B + s * CW + j * P
        eng.dma_start(keep["w_conv"][:, j % 2, :, s, :], w_v[:, :, at:at + P]).then_inc(sem, 16)


KC = (DC, CT, DC, 2)
KC_AT = (0, DC, DC + CT, 2 * DC + CT)


def load_mix(eng, io, keep, j, sem):
    w_v, co_v, ao_v = (io[x].rearrange("(c p) n -> p c n", p=P) for x in ("w_in", "w_conv_o", "w_attn_o"))
    for s, (v, col) in enumerate(((w_v, C_GC), (co_v, 0), (w_v, C_GA), (ao_v, 0))):
        eng.dma_start(keep["w_mix"][:, j % 2, KC_AT[s]:KC_AT[s] + KC[s], :],
                      v[:, :, col + j * P:col + (j + 1) * P]).then_inc(sem, 16)


def norm(nc, io, keep):
    with ExitStack() as ctx:
        n = Names(nc, ctx, "norm")
        XR = 3
        x, m, h = n.sb("x", [P, XR, D]), n.sb("m", [P, 2, D]), n.sb("h", [P, 2, D])
        sq = n.sb("sq", [P, D])
        gain, shift = n.sb("gain", [P, 2, D]), n.sb("shift", [P, 2, D])
        ss, rt, rs = n.sb("ss", [P, NT]), n.sb("rt", [P, NT]), n.sb("rs", [P, NT])
        psT = n.ps("psT", [P, 2, DC * P])
        x_in, rows_in = n.sems("x_loaded", XR), n.sem("rows_loaded")
        squared, rooted, inverted = n.sem("squared"), n.sem("rooted"), n.sem("inverted")
        scaled, shifted, turned, kept = n.sem("scaled"), n.sem("shifted"), n.sem("turned"), n.sem("kept")
        eps, eps_set = n.sb("eps", [P, 1]), n.sem("eps_set")
        maskf, mask_in, mask_set = n.sb("maskf", [P, NMASK * P]), n.sem("mask_loaded"), n.sem("mask_set")
        ahead = n.sem("loaded_ahead")
        hT = keep["hT"]
        G0, W, mod = ADA_FIRST, ADA_W, keep["mod"]
        psM = n.ps("psM", [P, 2, 512])
        wa_in, mm_done, mod_added = n.sems("w_ada_loaded", 2), n.sem("mm"), n.sem("mod_added")
        mod_scaled, mod_stored = n.sem("mod_scaled"), n.sem("mod_stored")
        block = ctx.enter_context(nc.Block())

        @block.sync
        def _(sp):
            for t in range(NT):
                R = rows_of(t)
                if t == XR:
                    sp.dma_start(maskf[:], io["pmask"]).then_inc(mask_in, 16)
                    for g in range(QKV_AHEAD):
                        load_qkv(sp, io, keep, g, ahead)
                if t >= XR:
                    sp.wait_ge(scaled, t - XR + 1)
                src = io["x_prompt"][t * P:t * P + R, :] if t < PT else io["x_sample"]
                sp.dma_start(x[0:R, t % XR, :], src).then_inc(x_in[t % XR], 16)
                if t == 0:
                    for i, tt in enumerate((0, PT)):
                        load_rows(sp, io, gain[:, i, :], tt, D, rows_in)
                        load_rows(sp, io, shift[:, i, :], tt, 0, rows_in)
            sp.wait_ge(ahead, 16 * QKV_AHEAD)
            sp.wait_ge(mod_scaled, 1)
            sp.dma_start(io["mod"][:, 2 * D:], mod[:, 2 * D:]).then_inc(mod_stored, 16)
            sp.wait_ge(mod_stored, 16)

        @block.gpsimd
        def _(pool):
            pool.memset(eps[:], EPS).then_inc(eps_set, 1)
            pool.tensor_copy(keep["identb"][:], keep["ident"][:]).then_inc(mask_set, 1)
            for g in range(G0 + 1, ADA_GROUPS):
                if g >= G0 + 2:
                    pool.wait_ge(mm_done, g - G0 - 1)
                if g == G0 + 4:
                    pool.wait_ge(mask_in, 16)
                    pool.tensor_copy(keep["mask"][:], maskf[:]).then_inc(mask_set, 1)
                load_ada(pool, io, keep, g, wa_in[g % 2])

        def keep_turned(act, t):
            R = rows_of(t)
            act.wait_ge(turned, t + 1)
            for i in range(2):
                src = psT[:, t % 2, i * 512:i * 512 + 4 * P].rearrange("p (c r) -> p c r", r=P)[:, :, 0:R]
                act.activation(hT[:, 4 * i:4 * i + 4, t * P:t * P + R], src, ACT.Copy).then_inc(kept, 1)

        @block.scalar
        def _(act):
            act.wait_ge(eps_set, 1)
            for t in range(NT):
                R = rows_of(t)
                act.wait_ge(x_in[t % XR], 16 * (t // XR + 1))
                if t:
                    act.wait_ge(squared, t)
                act.activation(sq[0:R, :], x[0:R, t % XR, :], ACT.Square,
                               accum_out=ss[0:R, t:t + 1]).then_inc(squared, 1)
                act.wait_ge(squared, t + 1)
                act.activation(rt[0:R, t:t + 1], ss[0:R, t:t + 1], ACT.Sqrt, bias=eps[0:R, :],
                               scale=1.0 / D).then_inc(rooted, 1)
                if t:
                    keep_turned(act, t - 1)
            keep_turned(act, NT - 1)

        @block.vector
        def _(dve):
            dve.wait_ge(rows_in, 64)
            for t in range(NT):
                R, i = rows_of(t), t // PT
                dve.wait_ge(rooted, t + 1)
                dve.reciprocal(rs[0:R, t:t + 1], rt[0:R, t:t + 1]).then_inc(inverted, 1)
                dve.wait_ge(inverted, t + 1)
                dve.scalar_tensor_tensor(out=m[0:R, t % 2, :], in0=x[0:R, t % XR, :], scalar=rs[0:R, t:t + 1],
                                         in1=gain[0:R, i, :], op0=ALU.mult, op1=ALU.mult).then_inc(scaled, 1)
                dve.wait_ge(scaled, t + 1)
                if t >= 2:
                    dve.wait_ge(turned, t - 1)
                dve.tensor_tensor(h[0:R, t % 2, :], m[0:R, t % 2, :], shift[0:R, i, :],
                                  ALU.add).then_inc(shifted, 1)
                if t < PT:
                    at = (G0 + t) * W
                    dve.wait_ge(mm_done, t + 1)
                    dve.tensor_tensor(mod[:, at:at + W], psM[0:NQ, t % 2, :], mod[:, at:at + W],
                                      ALU.add).then_inc(mod_added, 1)
            dve.wait_ge(mod_added, PT)
            dve.scalar_tensor_tensor(out=mod[:, 4 * D:5 * D], in0=mod[:, 4 * D:5 * D], scalar=1.0,
                                     in1=keep["gains"][:, 1, :], op0=ALU.add, op1=ALU.mult).then_inc(mod_scaled, 1)

        @block.tensor
        def _(pe):
            for t in range(NT):
                R = rows_of(t)
                if t < PT:
                    g = G0 + t
                    if t:
                        pe.wait_ge(wa_in[g % 2], 16 * ((t + 1) // 2))
                    if t >= 2:
                        pe.wait_ge(mod_added, t - 1)
                    project_ada(pe, keep, psM[0:NQ, t % 2, :], g).then_inc(mm_done, 1)
                pe.wait_ge(shifted, t + 1)
                if t >= 2:
                    pe.wait_ge(kept, 2 * (t - 1))
                for k in range(DC):
                    last = pe.transpose(psT[:, t % 2, k * P:k * P + R], h[0:R, t % 2, k * P:(k + 1) * P],
                                        keep["ident"][0:R, 0:R])
                last.then_inc(turned, 1)


def qkv(nc, io, keep):
    with ExitStack() as ctx:
        n = Names(nc, ctx, "qkv")
        W, ROT = WQKV, 4
        HB = W // HD
        NG = 3 * AW // W
        NR = 4 * NT
        slots = [x.rearrange("p (c n) -> p c n", c=DC) for x in keep["w_qkv"]]
        RING = len(slots)
        rope = n.sb("rope", [P, NT, 4 * (HD // 2)])
        m1, m2 = n.sb("m1", [P, 2, W]), n.sb("m2", [P, 2, W])
        rot = n.sb("rot", [P, ROT, W])
        psZ, psT = n.ps("psZ", [P, 3, 512]), n.ps("psT", [P, 2, 512])
        w_in, rope_in = n.sems("w_loaded", RING), n.sem("rope_loaded")
        z_done, m_done, rot_done = n.sem("z"), n.sem("m"), n.sem("rotated")
        v_kept, turned, kept = n.sem("v_kept"), n.sem("turned"), n.sem("kept")
        stored, v_stored = n.sems("stored", ROT), n.sem("v_stored")
        hT, V, Vs = keep["hT"], keep["V"], keep["Vs"]

        def heads(g):
            a, b = (g % 2) * W, (g % 2 + 1) * W
            return [(j, max(a, j * 256), min(b, (j + 1) * 256)) for j in range(GROUPS)
                    if max(a, j * 256) < min(b, (j + 1) * 256)]

        def store(eng, kv, t, j, a, b, src, sem):
            if t == PT:
                dst = io["kvs"][j][:, kv, a - j * 256:b - j * 256]
            else:
                first = (t * P) - (SEQ - CACHE_OUT[j])
                if first < 0:
                    return 0
                dst = io["kvp"][j][first:first + P, kv, a - j * 256:b - j * 256]
            eng.dma_start(dst, src).then_inc(sem, 16)
            return 1

        CACHE_OUT = tuple(min(x, SEQ) for x in WINDOWS)
        reads = [0] * ROT
        k_stores = {}
        for i in range(NR):
            g, t = divmod(i, NT)
            if g >= 2:
                reads[i % ROT] += sum(t == PT or t * P >= SEQ - CACHE_OUT[j] for j, _, _ in heads(g))
            k_stores[i] = reads[i % ROT]
        block = ctx.enter_context(nc.Block())

        @block.sync
        def _(sp):
            sp.dma_start(rope[:], io["rope"].rearrange("(t p) c -> p t c", p=P)).then_inc(rope_in, 16)
            for g in range(QKV_AHEAD, NG):
                if g >= RING:
                    sp.wait_ge(z_done, NT * (g - RING + 1))
                load_qkv(sp, io, keep, g, w_in[g % RING])
            count = 0
            for t in range(NT):
                sp.wait_ge(v_kept, NT + t + 1)
                for j in range(GROUPS):
                    src = V[:, t, j * 256:(j + 1) * 256] if t < PT else Vs[:, j * 256:(j + 1) * 256]
                    count += store(sp, 1, t, j, j * 256, (j + 1) * 256, src, v_stored)
            sp.wait_ge(v_stored, 16 * count)

        @block.gpsimd
        def _(pool):
            for i in range(2 * NT, NR):
                g, t = divmod(i, NT)
                R = rows_of(t)
                pool.wait_ge(rot_done, i + 1)
                for j, a, b in heads(g):
                    at = a - (g % 2) * W
                    store(pool, 0, t, j, a, b, rot[0:R, i % ROT, at:at + b - a], stored[i % ROT])
            for r in range(ROT):
                pool.wait_ge(stored[r], 16 * reads[r])

        @block.tensor
        def _(pe):
            def turn(i):
                g, t = divmod(i, NT)
                R = rows_of(t)
                pe.wait_ge(rot_done, i + 1)
                if i >= 2:
                    pe.wait_ge(kept, i - 1)
                for j in range(3):
                    last = pe.transpose(psT[:, i % 2, j * P:j * P + R], rot[0:R, i % ROT, j * P:(j + 1) * P],
                                        keep["ident"][0:R, 0:R])
                last.then_inc(turned, 1)

            for i in range(NG * NT):
                g, t = divmod(i, NT)
                R = rows_of(t)
                if t == 0 and g >= QKV_AHEAD:
                    pe.wait_ge(w_in[g % RING], 16 * (g // RING + (g % RING >= QKV_AHEAD)))
                if i >= 3:
                    if i - 3 < NR:
                        pe.wait_ge(m_done, 3 * (i - 2))
                    else:
                        pe.wait_ge(v_kept, i - 2 - NR)
                for k in range(DC):
                    last = pe.matmul(psZ[0:R, i % 3, 0:W], hT[:, k, t * P:t * P + R], slots[g % RING][:, k, :],
                                     start=(k == 0), stop=(k == DC - 1))
                last.then_inc(z_done, 1)
                if 1 <= i <= NR:
                    turn(i - 1)

        @block.vector
        def _(dve):
            dve.wait_ge(rope_in, 16)
            H = HD // 2
            for i in range(NR):
                g, t = divmod(i, NT)
                R = rows_of(t)
                z = psZ[0:R, i % 3, 0:W].rearrange("p (h d) -> p h d", d=HD)
                a = m1[0:R, i % 2, :].rearrange("p (h d) -> p h d", d=HD)
                b = m2[0:R, i % 2, :].rearrange("p (h d) -> p h d", d=HD)
                cos = rope[0:R, t:t + 1, 0:HD].broadcast_to([R, HB, HD])
                nsin = rope[0:R, t:t + 1, HD:HD + H].broadcast_to([R, HB, H])
                sin = rope[0:R, t:t + 1, HD + H:2 * HD].broadcast_to([R, HB, H])
                dve.wait_ge(z_done, i + 1)
                if i >= 2:
                    dve.wait_ge(rot_done, i - 1)
                dve.tensor_tensor(a, z, cos, ALU.mult).then_inc(m_done, 1)
                dve.tensor_tensor(b[:, :, 0:H], z[:, :, H:HD], nsin, ALU.mult).then_inc(m_done, 1)
                dve.tensor_tensor(b[:, :, H:HD], z[:, :, 0:H], sin, ALU.mult).then_inc(m_done, 1)
                dve.wait_ge(m_done, 3 * (i + 1))
                if i >= ROT:
                    dve.wait_ge(turned, i - ROT + 1)
                    if k_stores[i - ROT]:
                        dve.wait_ge(stored[i % ROT], 16 * k_stores[i - ROT])
                dve.tensor_tensor(rot[0:R, i % ROT, :], m1[0:R, i % 2, :], m2[0:R, i % 2, :],
                                  ALU.add).then_inc(rot_done, 1)

        @block.scalar
        def _(act):
            for i in range(NR):
                g, t = divmod(i, NT)
                R = rows_of(t)
                full, samp = (keep["qT"], keep["qTs"]) if g < 2 else (keep["kT"], keep["kTs"])
                pr = 3 * (g % 2)
                src = psT[:, i % 2, 0:3 * P].rearrange("p (j r) -> p j r", r=P)[:, :, 0:R]
                dst = full[:, pr:pr + 3, t * P:(t + 1) * P] if t < PT else samp[:, pr:pr + 3, :]
                act.wait_ge(turned, i + 1)
                act.activation(dst, src, ACT.Copy).then_inc(kept, 1)
            for i in range(NR, NG * NT):
                g, t = divmod(i, NT)
                R = rows_of(t)
                at = (g - 4) * W
                dst = V[:, t, at:at + W] if t < PT else Vs[:, at:at + W]
                act.wait_ge(z_done, i + 1)
                act.activation(dst, psZ[0:R, i % 3, 0:W], ACT.Copy).then_inc(v_kept, 1)


def attend(nc, io, keep):
    with ExitStack() as ctx:
        n = Names(nc, ctx, "att")
        NI = PT * SLOTS
        NB = sum(BLOCKS)
        TR = 4
        mask, identb = keep["mask"], keep["identb"]
        prob = n.sb("prob", [P, 2, NB * P])
        pT = keep["pT"]
        o = n.sb("o", [P, 2, SLOTS * HD])
        mx, nm, den, rden = (n.sb(x, [P, NI]) for x in ("mx", "nm", "den", "rden"))
        psS, psT, psO = n.ps("psS", [P, 4 * 512]), n.ps("psT", [P, 2, 512]), n.ps("psO", [P, 2, 512])
        scored, maxed, negated, expd = n.sem("scored"), n.sem("maxed"), n.sem("negated"), n.sem("exp")
        inverted, turned, summed = n.sem("inverted"), n.sem("turned"), n.sem("summed")
        kept_act, kept_dve = n.sem("kept_by_act"), n.sem("kept_by_dve")
        scaled, o_turned, o_kept = n.sem("scaled"), n.sem("o_turned"), n.sem("o_kept")
        qT, kT, V, oT, ident = keep["qT"], keep["kT"], keep["V"], keep["oT"], keep["ident"]
        blocks = [key_blocks(it // SLOTS) for it in range(NI)]
        first = [0]
        for b in blocks:
            first.append(first[-1] + -(-len(b) // 4))
        ACT_B = 2
        carrier, by_act, by_dve = [], 0, 0
        for it in range(NI):
            for j in range(first[it + 1] - first[it]):
                if j < ACT_B:
                    by_act += 1
                    carrier.append((kept_act, by_act))
                else:
                    by_dve += 1
                    carrier.append((kept_dve, by_dve))

        def carry(eng, it, mine, copy):
            for b in range(first[it], first[it + 1]):
                if mine(b - first[it]):
                    m = min(4, len(blocks[it]) - 4 * (b - first[it]))
                    eng.wait_ge(turned, b + 1)
                    if b >= TR:
                        eng.wait_ge(summed, b - TR + 1)
                    copy(pT[:, b % TR, 0:m * P], psT[:, b % 2, 0:m * P]).then_inc(carrier[b][0], 1)

        block = ctx.enter_context(nc.Block())

        @block.tensor
        def _(pe):
            def scores(it):
                t, h = divmod(it, SLOTS)
                lane = HD * (h % 2)
                if it:
                    pe.wait_ge(expd, it)
                bl, at = blocks[it], 0
                while at < len(bl):
                    g, kb = bl[at]
                    run = 1
                    while at + run < len(bl) and bl[at + run][0] == g and (at + run) % 4:
                        run += 1
                    dst = psS[:, at * P:(at + run) * P]
                    m0 = mask_block(g, t, kb)
                    pe.matmul(dst, identb[:], mask[:, m0 * P:(m0 + run) * P], start=True, stop=False)
                    pair = 2 * g + h // 2
                    last = pe.matmul(dst, qT[lane:lane + HD, pair, t * P:(t + 1) * P],
                                     kT[lane:lane + HD, pair, kb * P:(kb + run) * P], start=False, stop=True)
                    at += run
                last.then_inc(scored, 1)

            def outputs(it):
                t, h = divmod(it, SLOTS)
                bl = blocks[it]
                NBT = first[it + 1] - first[it]
                pe.wait_ge(expd, it + 1)

                def turn(j):
                    b = first[it] + j
                    if b >= 2:
                        pe.wait_ge(*carrier[b - 2])
                    for i in range(4 * j, min(4 * j + 4, len(bl))):
                        last = pe.transpose(psT[:, b % 2, (i % 4) * P:(i % 4 + 1) * P],
                                            prob[:, it % 2, i * P:(i + 1) * P], ident[:])
                    last.then_inc(turned, 1)

                def weigh(j):
                    b = first[it] + j
                    pe.wait_ge(*carrier[b])
                    if it >= 2 and j == 0:
                        pe.wait_ge(scaled, it - 1)
                        if it % 2 and t and h == 1:
                            pe.wait_ge(o_kept, t)
                    for i in range(4 * j, min(4 * j + 4, len(bl))):
                        g, kb = bl[i]
                        last = pe.matmul(psO[:, it % 2, 0:HD], pT[:, b % TR, (i % 4) * P:(i % 4 + 1) * P],
                                         V[:, kb, (g * SLOTS + h) * HD:(g * SLOTS + h + 1) * HD],
                                         start=(i == 0), stop=(i == len(bl) - 1))
                    last.then_inc(summed, 1)

                for j in range(NBT + 2):
                    if j < NBT:
                        turn(j)
                    if j >= 2:
                        weigh(j - 2)

            def turn_o(t):
                pe.wait_ge(scaled, SLOTS * (t + 1))
                for j in range(2):
                    last = pe.transpose(psO[:, 1, j * P:(j + 1) * P], o[:, t % 2, j * P:(j + 1) * P],
                                        ident[:])
                last.then_inc(o_turned, 1)

            scores(0)
            for it in range(NI):
                if it + 1 < NI:
                    scores(it + 1)
                outputs(it)
                if it >= 1 and (it - 1) % SLOTS == SLOTS - 1:
                    turn_o((it - 1) // SLOTS)
            turn_o(PT - 1)

        @block.vector
        def _(dve):
            def top(it):
                dve.wait_ge(scored, it + 1)
                dve.tensor_reduce(mx[:, it:it + 1], psS[:, 0:len(blocks[it]) * P], AX, ALU.max).then_inc(maxed, 1)
                dve.wait_ge(maxed, it + 1)
                dve.tensor_scalar(nm[:, it:it + 1], mx[:, it:it + 1], -SCALE, None, ALU.mult).then_inc(negated, 1)

            top(0)
            for it in range(NI):
                if it + 1 < NI:
                    top(it + 1)
                dve.wait_ge(expd, it + 1)
                dve.reciprocal(rden[:, it:it + 1], den[:, it:it + 1]).then_inc(inverted, 1)
                carry(dve, it, lambda j: j >= ACT_B, dve.tensor_copy)

        @block.scalar
        def _(act):
            def exps(it):
                act.wait_ge(negated, it + 1)
                m = len(blocks[it]) * P
                if it >= 2:
                    act.wait_ge(turned, first[it - 1])
                act.activation(prob[:, it % 2, 0:m], psS[:, 0:m], ACT.Exp, bias=nm[:, it:it + 1], scale=SCALE,
                               accum_out=den[:, it:it + 1]).then_inc(expd, 1)

            def keep_o(t):
                act.wait_ge(o_turned, t + 1)
                act.activation(oT[:, :, t * P:(t + 1) * P],
                               psO[:, 1, 0:2 * P].rearrange("p (j r) -> p j r", r=P),
                               ACT.Copy).then_inc(o_kept, 1)

            exps(0)
            for it in range(NI):
                carry(act, it, lambda j: j < ACT_B, lambda out, src: act.activation(out, src, ACT.Copy))
                if it + 1 < NI:
                    exps(it + 1)
                t, h = divmod(it, SLOTS)
                act.wait_ge(summed, first[it + 1])
                act.wait_ge(inverted, it + 1)
                if t >= 2 and h == 0:
                    act.wait_ge(o_turned, t - 1)
                act.activation(o[:, t % 2, h * HD:(h + 1) * HD], psO[:, it % 2, 0:HD], ACT.Copy,
                               scale=rden[:, it:it + 1]).then_inc(scaled, 1)
                if it >= 1 and (it - 1) % SLOTS == SLOTS - 1:
                    keep_o((it - 1) // SLOTS)
            keep_o(PT - 1)


def sampled(nc, io, keep):
    with ExitStack() as ctx:
        n = Names(nc, ctx, "smp")
        QB = 4
        NB6 = 6
        K, Vc = n.sb("K", [P, 2, SBLK, 256]), n.sb("Vc", [P, QB, SBLK, 256])
        kTc = n.sb("kTc", [P, 2, 2, SNEW])
        qz = n.sb("qz", [P, GROUPS, QB, 2, P])
        mask, S, pr = n.sb("mask", [P, SCOLS]), n.sb("S", [P, SCOLS]), n.sb("pr", [P, SCOLS])
        pT = n.sb("pT", [P, SBLK + GROUPS, P])
        mx, nm, den, rden = (n.sb(x, [P, 2]) for x in ("mx", "nm", "den", "rden"))
        psS, psT, psO = n.ps("psS", [P, 3 * 512]), n.ps("psT", [P, 3, 512]), n.ps("psO", [P, 2, 512])
        o_rows = n.sb("o_rows", [SLOTS * NEW, QB, 256])
        k_in, v_in, mask_in = n.sems("k_loaded", 2), n.sems("v_loaded", QB), n.sem("mask_loaded")
        q_clear, q_set = n.sem("q_clear"), n.sems("q_set", QB)
        k_turned, k_kept, scored = n.sem("k_turned"), n.sem("k_kept"), n.sem("scored")
        scored_part = n.sem("scored_part")
        masked, maxed, negated, expd = n.sem("masked"), n.sem("maxed"), n.sem("negated"), n.sem("exp")
        inverted, normed, p_turned, p_kept = n.sem("inverted"), n.sem("normed"), n.sem("p_turned"), n.sem("p_kept")
        weighed, rows_kept = n.sem("weighed"), n.sem("rows_kept")
        summed, o_kept = n.sem("summed"), n.sem("o_kept")
        qTs, kTs, Vs, oT, ident = keep["qTs"], keep["kTs"], keep["Vs"], keep["oT"], keep["ident"]
        BG = [1] * 4 + [2] * 4 + [0]

        def load(eng, b, kv, dst, sem):
            c0, c1, c2 = io["cache"]
            eng.dma_start(dst[:, 0:4, :], c1[b, :, kv, :].rearrange("(p j) c -> p j c", j=4)).then_inc(sem, 16)
            for s in range(2):
                src = bass.AP(c2.tensor, c2.offset + ((b * CACHE[2] + 4 * s) * 2 + kv) * 256,
                              [[16 * 512, 64], [512, 4], [1, 256]])
                eng.dma_start(dst[64 * s:64 * s + 64, 4:8, :], src).then_inc(sem, 16)
            eng.dma_start(dst[:, 8, :], c0[b, :, kv, :]).then_inc(sem, 16)

        ahead = n.sem("loaded_ahead")
        block = ctx.enter_context(nc.Block())
        TB = 3

        def place_q(r, copy):
            for b in range(QB):
                for g in range(GROUPS):
                    for h in range(SLOTS):
                        lane, pair = HD * (h % 2), h // 2
                        at = b * 32 + h * NEW
                        tok = (QB * r + b) * NEW
                        copy(qz[lane:lane + HD, g, b, pair, at:at + NEW],
                             qTs[lane:lane + HD, 2 * g + pair, tok:tok + NEW]).then_inc(q_set[b], 1)

        @block.sync
        def _(sp):
            for b in range(NSEQ):
                if b >= 2:
                    sp.wait_ge(k_turned, NB6 * (b - 1))
                load(sp, b, 0, K[:, b % 2], k_in[b % 2])
                if b in (1, QB + 1):
                    if b > QB:
                        sp.wait_ge(masked, 1)
                    sp.dma_start(mask[:], io["smask"][b // QB]).then_inc(mask_in, 16)
            for j in range(2):
                load_conv(sp, io, keep, j, ahead)
            sp.wait_ge(ahead, 96)

        @block.gpsimd
        def _(pool):
            for r in range(2):
                if r:
                    pool.wait_ge(scored, 1)
                    place_q(1, pool.tensor_copy)
                for b in range(QB):
                    if r:
                        pool.wait_ge(summed, 1)
                    load(pool, QB * r + b, 1, Vc[:, b], v_in[b])

        KEPT = (NB6 * (QB + 2), NB6 * NSEQ)

        @block.tensor
        def _(pe):
            def turn_keys(b):
                pe.wait_ge(k_in[b % 2], 64 * (b // 2 + 1))
                for pair in range(2):
                    for j in range(3):
                        i = NB6 * b + 3 * pair + j
                        if i >= 3:
                            pe.wait_ge(k_kept, i - 2)
                        for k in range(4 * j, min(4 * j + 4, SBLK)):
                            last = pe.transpose(psT[:, i % 3, (k % 4) * P:(k % 4 + 1) * P],
                                                K[:, b % 2, k, pair * P:(pair + 1) * P], ident[:])
                        last.then_inc(k_turned, 1)

            def scores(b):
                q, r = b % QB, b // QB
                pe.wait_ge(k_kept, NB6 * (b + 1))
                pe.wait_ge(q_set[q], GROUPS * SLOTS * (r + 1))
                if q == 0 and r:
                    pe.wait_ge(masked, 1)
                for pair in range(2):
                    for at, m, g in ((0, 4, 1), (4, 4, 2), (8, 1, 0)):
                        last = pe.matmul(psS[:, at * P:(at + m) * P], qz[:, g, q, pair, :],
                                         kTc[:, b % 2, pair, at * P:(at + m) * P],
                                         start=(q == 0 and pair == 0), stop=(q == QB - 1 and pair == 1))
                if q == QB - 1:
                    for g in range(GROUPS):
                        for q2 in range(QB):
                            for pair in range(2):
                                last = pe.matmul(psS[:, SNEW + g * NS:SNEW + (g + 1) * NS],
                                                 qz[:, g, q2, pair, :], kTs[:, 2 * g + pair, :],
                                                 start=(q2 == 0 and pair == 0), stop=(q2 == QB - 1 and pair == 1))
                    last.then_inc(scored, 1)
                else:
                    last.then_inc(scored_part, 1)

            def outputs(r):
                pe.wait_ge(normed, r + 1)
                for j in range(TB):
                    if j == 0:
                        pe.wait_ge(k_kept, KEPT[r])
                    for k in range(4 * j, 4 * j + 4):
                        if k < SBLK:
                            last = pe.transpose(psT[:, j, (k % 4) * P:(k % 4 + 1) * P], pr[:, k * P:(k + 1) * P],
                                                ident[:])
                        else:
                            g = k - SBLK
                            last = pe.transpose(psT[0:NS, j, (k % 4) * P:(k % 4 + 1) * P],
                                                pr[:, SNEW + g * NS:SNEW + (g + 1) * NS], ident[:])
                    last.then_inc(p_turned, 1)
                pe.wait_ge(p_kept, (TB + 1) * (r + 1))
                if r:
                    pe.wait_ge(o_kept, 4)
                RW = SLOTS * NEW
                for q in range(QB):
                    pe.wait_ge(v_in[q], 64 * (r + 1))
                    dst = psO[0:RW, q // 2, q % 2 * 256:(q % 2 + 1) * 256]
                    for k in range(SBLK):
                        pe.matmul(dst, pT[:, k, q * RW:(q + 1) * RW], Vc[:, q, k, :], start=(k == 0), stop=False)
                    for g in range(GROUPS):
                        last = pe.matmul(dst, pT[0:NS, SBLK + g, q * RW:(q + 1) * RW], Vs[:, g * 256:(g + 1) * 256],
                                         start=False, stop=(g == GROUPS - 1))
                    if q % 2:
                        last.then_inc(weighed, 1)
                pe.wait_ge(rows_kept, 2 * (r + 1))
                for q in range(QB):
                    for pair in range(2):
                        last = pe.transpose(psO[:, 0, (2 * q + pair) * RW:(2 * q + pair + 1) * RW],
                                            o_rows[:, q, pair * P:(pair + 1) * P], ident[0:RW, 0:RW])
                last.then_inc(summed, 1)

            turn_keys(0)
            for b in range(NSEQ):
                if b + 1 < NSEQ:
                    turn_keys(b + 1)
                scores(b)
                if b == QB:
                    outputs(0)
            outputs(1)

        @block.vector
        def _(dve):
            def keep_keys(b):
                if b >= 2:
                    dve.wait_ge(scored_part, (b - 2) // QB * (QB - 1) + min((b - 2) % QB + 1, QB - 1))
                    if b >= QB + 1:
                        dve.wait_ge(scored, 1)
                for pair in range(2):
                    for j in range(3):
                        i = NB6 * b + 3 * pair + j
                        m = 4 if j < 2 else 1
                        dve.wait_ge(k_turned, i + 1)
                        dve.tensor_copy(kTc[:, b % 2, pair, 4 * j * P:(4 * j + m) * P],
                                        psT[:, i % 3, 0:m * P]).then_inc(k_kept, 1)

            def top(r):
                dve.wait_ge(scored, r + 1)
                dve.wait_ge(mask_in, 16 * (r + 1))
                if r:
                    dve.wait_ge(expd, r)
                dve.tensor_tensor(S[:], psS[:, 0:SCOLS], mask[:], ALU.add).then_inc(masked, 1)
                dve.wait_ge(masked, r + 1)
                dve.tensor_reduce(mx[:, r:r + 1], S[:], AX, ALU.max).then_inc(maxed, 1)
                dve.wait_ge(maxed, r + 1)
                dve.tensor_scalar(nm[:, r:r + 1], mx[:, r:r + 1], -SCALE, None, ALU.mult).then_inc(negated, 1)

            def probs(r):
                dve.wait_ge(expd, r + 1)
                dve.reciprocal(rden[:, r:r + 1], den[:, r:r + 1]).then_inc(inverted, 1)
                dve.wait_ge(inverted, r + 1)
                dve.tensor_scalar(pr[:], pr[:], rden[:, r:r + 1], None, ALU.mult).then_inc(normed, 1)
                for j in range(TB):
                    dve.wait_ge(p_turned, TB * r + j + 1)
                    if j == 0 and r:
                        dve.wait_ge(summed, r)
                    if j < 2:
                        dve.tensor_copy(pT[:, 4 * j:4 * j + 4, :].rearrange("p j c -> p (j c)"),
                                        psT[:, j, :]).then_inc(p_kept, 1)
                    else:
                        dve.tensor_copy(pT[:, 8, :], psT[:, j, 0:P]).then_inc(p_kept, 1)
                        dve.tensor_copy(pT[0:NS, 9:12, :].rearrange("p j c -> p (j c)"),
                                        psT[0:NS, j, P:4 * P]).then_inc(p_kept, 1)

            def keep_o(r):
                dve.wait_ge(summed, r + 1)
                for pair in range(2):
                    for e in range(2):
                        lane, h = HD * e, 2 * pair + e
                        src = psO[lane:lane + HD, 0, 0:QB * 64].rearrange("p (q c) -> p q c", c=64)[
                            :, :, pair * 32 + h * NEW:pair * 32 + (h + 1) * NEW]
                        at = SEQ + QB * r * NEW
                        dst = oT[lane:lane + HD, pair, at:at + QB * NEW].rearrange("p (q i) -> p q i", i=NEW)
                        dve.tensor_copy(dst, src).then_inc(o_kept, 1)

            dve.memset(qz[:], 0.0).then_inc(q_clear, 1)
            for b in range(QB + 1):
                keep_keys(b)
            top(0)
            keep_keys(QB + 1)
            probs(0)
            keep_keys(QB + 2)
            keep_o(0)
            keep_keys(QB + 3)
            top(1)
            probs(1)
            keep_o(1)

        @block.scalar
        def _(act):
            act.wait_ge(q_clear, 1)
            place_q(0, lambda out, src: act.activation(out, src, ACT.Copy))
            for r in range(2):
                act.wait_ge(negated, r + 1)
                if r:
                    act.wait_ge(p_turned, TB * r)
                act.activation(pr[:], S[:], ACT.Exp, bias=nm[:, r:r + 1], scale=SCALE,
                               accum_out=den[:, r:r + 1]).then_inc(expd, 1)
                for i in range(2):
                    act.wait_ge(weighed, 2 * r + i + 1)
                    act.activation(o_rows[:, 2 * i:2 * i + 2, :].rearrange("p q c -> p (q c)"),
                                   psO[0:SLOTS * NEW, i, :], ACT.Copy).then_inc(rows_kept, 1)


SEGS = ((0, 3 * P), (3 * P, 3 * P), (6 * P, TOK - 6 * P))


TAIL = 2 + 2 * NSEQ


def conv(nc, io, keep):
    with ExitStack() as ctx:
        n = Names(nc, ctx, "conv")
        NI = CT * 3
        w = keep["w_conv"]
        RS = 2 * NSEQ + 3
        stT = n.sb("stT", [P, CT, RS])
        spare = keep["spare"]
        up = spare[:, 0:2 * (2 + SEQ)].rearrange("p (s c) -> p s c", s=2)
        rest = spare[:, 2 * (2 + SEQ):]
        state = rest[0:RS, 0:CW]
        us = n.sb("us", [P, 2, NSEQ, 2 + NEW])
        cg, y0, y1 = n.sb("cg", [P, 2, 512]), n.sb("y0", [P, 2, 512]), n.sb("y1", [P, 2, 512])
        y2 = y0
        tail = keep["tail"]
        psZ, psT = n.ps("psZ", [P, 2, 3, 512]), n.ps("psT", [P, 1, 512])
        w_in, small_in = n.sems("w_loaded", 2), n.sem("state_loaded")
        st_turned, st_kept, z_done = n.sem("st_turned"), n.sem("st_kept"), n.sem("z")
        c_kept, padded, u_done = n.sem("c_kept"), n.sem("padded"), n.sem("u")
        y_done, gated, tail_set = n.sem("y"), n.sem("gated"), n.sem("tail_set")
        ahead = n.sem("loaded_ahead")
        hT, zT, ident = keep["hT"], keep["zT"], keep["ident"]

        def pieces(s):
            a, m = SEGS[s]
            return [(a, m, 0)] if a + m <= SEQ else [(a, SEQ - a, 0), (SEQ, NS, SEQ - a)]

        def pieces_before(i):
            return (len(SEGS) + 1) * (i // 3) + i % 3

        block = ctx.enter_context(nc.Block())

        @block.sync
        def _(sp):
            sp.dma_start(state[0:2 * NSEQ, :], io["state_conv"]).then_inc(small_in, 16)
            sp.dma_start(state[2 * NSEQ:RS, :], io["conv_w"]).then_inc(small_in, 16)
            for j in range(2, CT):
                sp.wait_ge(z_done, 3 * (j - 1))
                load_conv(sp, io, keep, j, w_in[j % 2])
            for j in range(2):
                load_mix(sp, io, keep, j, ahead)
            sp.wait_ge(ahead, 128)

        @block.tensor
        def _(pe):
            for i in range(NI):
                j, s = divmod(i, 3)
                a, m = SEGS[s]
                if i == 1:
                    pe.wait_ge(small_in, 32)
                    for c in range(CT):
                        last = pe.transpose(psT[:, 0, c * RS:(c + 1) * RS], state[:, c * P:(c + 1) * P],
                                            ident[0:RS, 0:RS])
                    last.then_inc(st_turned, 1)
                if s == 0 and j >= 2:
                    pe.wait_ge(w_in[j % 2], 48 * (j // 2))
                if i >= 2:
                    pe.wait_ge(gated, pieces_before(i - 1))
                for part in (1, 2, 0):
                    for k in range(DC):
                        last = pe.matmul(psZ[:, i % 2, part, 0:m], w[:, j % 2, k, part, :], hT[:, k, a:a + m],
                                         start=(k == 0), stop=(k == DC - 1))
                last.then_inc(z_done, 1)

        @block.scalar
        def _(act):
            act.wait_ge(st_turned, 1)
            act.activation(stT[:].rearrange("p j c -> p (j c)"), psT[:, 0, 0:CT * RS], ACT.Copy).then_inc(st_kept, 1)
            for i in range(NI):
                j, s = divmod(i, 3)
                m = SEGS[s][1]
                act.wait_ge(z_done, i + 1)
                if i >= 2:
                    act.wait_ge(u_done, pieces_before(i - 1))
                act.activation(cg[:, i % 2, 0:m], psZ[:, i % 2, 1, 0:m], ACT.Copy).then_inc(c_kept, 1)

        @block.vector
        def _(dve):
            for s in range(2):
                dve.memset(up[:, s, 0:2], 0.0).then_inc(padded, 1)
            dve.wait_ge(padded, 2)
            dve.wait_ge(st_kept, 1)
            for i in range(NI):
                j, s = divmod(i, 3)
                for p, (a, m, off) in enumerate(pieces(s)):
                    q = pieces_before(i) + p
                    if a < SEQ:
                        U = lambda d: up[:, j % 2, 2 + a - d:2 + a - d + m]
                        shape = lambda ap: ap
                    else:
                        U = lambda d: us[:, j % 2, :, 2 - d:2 - d + NEW]
                        shape = lambda ap: ap.rearrange("p (b i) -> p b i", i=NEW)
                        dve.tensor_copy(us[:, j % 2, :, 0:2], stT[:, j, 0:2 * NSEQ].rearrange(
                            "p (b k) -> p b k", k=2)).then_inc(padded, 1)
                    cols = slice(off, off + m)
                    dve.wait_ge(c_kept, i + 1)
                    dve.tensor_tensor(U(0), shape(cg[:, i % 2, cols]), shape(psZ[:, i % 2, 2, cols]),
                                      ALU.mult).then_inc(u_done, 1)
                    dve.wait_ge(u_done, q + 1)
                    dve.wait_ge(padded, 2 + j + (a >= SEQ))
                    if i >= 2:
                        dve.wait_ge(gated, pieces_before(i - 1))
                    dve.tensor_scalar(shape(y0[:, i % 2, cols]), U(2), stT[:, j, 2 * NSEQ:2 * NSEQ + 1], None,
                                      ALU.mult).then_inc(y_done, 1)
                    dve.wait_ge(y_done, 3 * q + 1)
                    dve.scalar_tensor_tensor(out=shape(y1[:, i % 2, cols]), in0=U(1),
                                             scalar=stT[:, j, 2 * NSEQ + 1:2 * NSEQ + 2],
                                             in1=shape(y0[:, i % 2, cols]), op0=ALU.mult,
                                             op1=ALU.add).then_inc(y_done, 1)
                    dve.wait_ge(y_done, 3 * q + 2)
                    dve.scalar_tensor_tensor(out=shape(y2[:, i % 2, cols]), in0=U(0),
                                             scalar=stT[:, j, 2 * NSEQ + 2:2 * NSEQ + 3],
                                             in1=shape(y1[:, i % 2, cols]), op0=ALU.mult,
                                             op1=ALU.add).then_inc(y_done, 1)
                    dve.wait_ge(y_done, 3 * q + 3)
                    dve.tensor_tensor(zT[:, j, a:a + m], y2[:, i % 2, cols], psZ[:, i % 2, 0, cols],
                                      ALU.mult).then_inc(gated, 1)
                    if a + m == SEQ:
                        dve.tensor_copy(tail[:, j, 0:2], up[:, j % 2, SEQ:SEQ + 2]).then_inc(tail_set, 1)
                    if a >= SEQ:
                        dve.tensor_copy(tail[:, j, 2:TAIL].rearrange("p (b k) -> p b k", k=2),
                                        us[:, j % 2, :, NEW:NEW + 2]).then_inc(tail_set, 1)


def mix(nc, io, keep):
    with ExitStack() as ctx:
        n = Names(nc, ctx, "mix")
        NI = DC * 3
        AT, w = KC_AT, keep["w_mix"]
        sg, br = n.sb("sg", [P, 2, 2, 512]), n.sb("br", [P, 2, 2, 512])
        psZ = n.ps("psZ", [P, 2, 4, 512])
        w_in = n.sems("w_loaded", 2)
        z_done, gates, weighed, mixed = n.sem("z"), n.sem("gates"), n.sem("weighed"), n.sem("mixed")
        hT, zT, oT, mT = keep["hT"], keep["zT"], keep["oT"], keep["mT"]
        ahead = n.sem("loaded_ahead")
        block = ctx.enter_context(nc.Block())

        @block.sync
        def _(sp):
            wo_v = io["w_o"].rearrange("(c p) n -> p c n", p=P)
            for j in range(2, DC):
                sp.wait_ge(z_done, 3 * (j - 1))
                load_mix(sp, io, keep, j, w_in[j % 2])
            sp.dma_start(keep["w_out"], wo_v).then_inc(ahead, 16)
            sp.wait_ge(ahead, 16)

        @block.tensor
        def _(pe):
            for i in range(NI):
                j, s = divmod(i, 3)
                a, m = SEGS[s]
                if s == 0 and j >= 2:
                    pe.wait_ge(w_in[j % 2], 64 * (j // 2))
                if i >= 2:
                    pe.wait_ge(weighed, 2 * (i - 1))
                for q, src in enumerate((hT, zT, hT, oT)):
                    for k in range(KC[q]):
                        last = pe.matmul(psZ[:, i % 2, q, 0:m], w[:, j % 2, AT[q] + k, :], src[:, k, a:a + m],
                                         start=(k == 0), stop=(k == KC[q] - 1))
                last.then_inc(z_done, 1)

        @block.scalar
        def _(act):
            for i in range(NI):
                m = SEGS[i % 3][1]
                act.wait_ge(z_done, i + 1)
                if i >= 2:
                    act.wait_ge(weighed, 2 * (i - 1))
                for q in range(2):
                    act.activation(sg[:, i % 2, q, 0:m], psZ[:, i % 2, 2 * q, 0:m], ACT.Sigmoid).then_inc(gates, 1)

        @block.vector
        def _(dve):
            for i in range(NI):
                j, s = divmod(i, 3)
                a, m = SEGS[s]
                dve.wait_ge(gates, 2 * (i + 1))
                if i >= 2:
                    dve.wait_ge(mixed, i - 1)
                for q in range(2):
                    dve.tensor_tensor(br[:, i % 2, q, 0:m], sg[:, i % 2, q, 0:m], psZ[:, i % 2, 2 * q + 1, 0:m],
                                      ALU.mult).then_inc(weighed, 1)
                dve.wait_ge(weighed, 2 * (i + 1))
                dve.tensor_tensor(mT[:, j, a:a + m], br[:, i % 2, 0, 0:m], br[:, i % 2, 1, 0:m],
                                  ALU.add).then_inc(mixed, 1)


def out(nc, io, keep):
    with ExitStack() as ctx:
        n = Names(nc, ctx, "out")
        w = keep["w_out"]
        gate, x, y, x1 = n.sb("gate", [P, 2, D]), n.sb("x", [P, 2, D]), n.sb("y", [P, 2, D]), n.sb("x1", [P, 2, D])
        psM, psT = n.ps("psM", [P, 2, D]), n.ps("psT", [P, 2, 512])
        tail, tailT = keep["tail"], n.sb("tailT", [TAIL, CW])
        t_turned, t_kept, t_stored = n.sem("t_turned"), n.sem("t_kept"), n.sem("t_stored")
        x_in, rows_in, ahead = n.sems("x_loaded", 2), n.sem("rows_loaded"), n.sem("loaded_ahead")
        projected, gated, added, stored = n.sem("projected"), n.sem("gated"), n.sem("added"), n.sems("stored", 2)
        mT = keep["mT"]
        wq_v = io["w_query"].rearrange("(c p) n -> p c n", p=P)
        block = ctx.enter_context(nc.Block())

        @block.sync
        def _(sp):
            for i, t in enumerate((0, PT)):
                load_rows(sp, io, gate[:, i, :], t, 2 * D, rows_in)
            for t in range(NT):
                R = rows_of(t)
                if t >= 2:
                    sp.wait_ge(added, t - 1)
                src = io["x_prompt"][t * P:t * P + R, :] if t < PT else io["x_sample"]
                sp.dma_start(x[0:R, t % 2, :], src).then_inc(x_in[t % 2], 16)
                if 1 <= t <= 2:
                    sp.dma_start(keep["wq"][:, :, (t - 1) * D:t * D], wq_v[:, :, (t - 1) * D:t * D]).then_inc(ahead, 16)
            sp.wait_ge(t_kept, 2)
            sp.dma_start(io["conv_prompt"], tailT[0:2, :]).then_inc(t_stored, 16)
            sp.dma_start(io["conv_sample"], tailT[2:TAIL, :]).then_inc(t_stored, 16)
            sp.wait_ge(t_stored, 32)
            sp.wait_ge(ahead, 32)

        @block.scalar
        def _(act):
            act.wait_ge(t_turned, 1)
            act.activation(tailT[:, 0:512], psT[0:TAIL, 0, :], ACT.Copy).then_inc(t_kept, 1)
            act.activation(tailT[:, 512:CW], psT[0:TAIL, 1, 0:CW - 512], ACT.Copy).then_inc(t_kept, 1)

        @block.gpsimd
        def _(pool):
            for t in range(NT):
                R = rows_of(t)
                pool.wait_ge(added, t + 1)
                pool.dma_start(io["x1"][t * P:t * P + R, :], x1[0:R, t % 2, :]).then_inc(stored[t % 2], 16)
            pool.wait_ge(stored[0], 16 * 5)
            pool.wait_ge(stored[1], 16 * 4)

        @block.tensor
        def _(pe):
            for t in range(NT):
                R = rows_of(t)
                if t >= 2:
                    pe.wait_ge(gated, t - 1)
                for i in range(2):
                    for k in range(DC):
                        last = pe.matmul(psM[0:R, t % 2, i * 512:(i + 1) * 512], mT[:, k, t * P:t * P + R],
                                         w[:, k, i * 512:(i + 1) * 512], start=(k == 0), stop=(k == DC - 1))
                last.then_inc(projected, 1)
                if t == 0:
                    for j in range(CT):
                        last = pe.transpose(psT[0:TAIL, j // 4, (j % 4) * P:(j % 4 + 1) * P], tail[:, j, :],
                                            keep["ident"][:])
                    last.then_inc(t_turned, 1)

        @block.vector
        def _(dve):
            dve.wait_ge(rows_in, 32)
            for t in range(NT):
                R = rows_of(t)
                dve.wait_ge(projected, t + 1)
                if t >= 2:
                    dve.wait_ge(added, t - 1)
                dve.tensor_tensor(y[0:R, t % 2, :], psM[0:R, t % 2, :], gate[0:R, t // PT, :],
                                  ALU.mult).then_inc(gated, 1)
                dve.wait_ge(gated, t + 1)
                dve.wait_ge(x_in[t % 2], 16 * (t // 2 + 1))
                if t >= 2:
                    dve.wait_ge(stored[t % 2], 16 * (t // 2))
                dve.tensor_tensor(x1[0:R, t % 2, :], y[0:R, t % 2, :], x[0:R, t % 2, :], ALU.add).then_inc(added, 1)

def wait_apart(eng, sem, value, passed):
    eng.wait_ge(sem, value)
    if not isinstance(value, int):
        eng.sem_inc(passed, 1)


class Link:

    def __init__(self, eng, sem):
        self.eng, self.sem, self.n = eng, sem, 0

    def __call__(self, ins):
        ins.then_inc(self.sem, 1)
        self.n += 1

    def wait(self):
        self.eng.wait_ge(self.sem, self.n)

    def restart(self):
        self.wait()
        self.eng.sem_clear(self.sem)
        self.n = 0


def peer(nc, io, keep):
    with ExitStack() as ctx:
        n = Names(nc, ctx, "peer")
        U, K2 = 8, 2 * KEYS
        V2, HALF = U // 2, TOPK // 2
        LAST = NT * HEADS
        wq = keep["wq"]
        sk, skT = n.sb("sk", [P, 2, P]), n.sb("skT", [P, 2, P])
        gain, shift, gate2, gainf = (n.sb(x, [P, D]) for x in ("gain", "shift", "gate2", "gainf"))
        xp, xf, m, h2n, h2 = (n.sb(x, [P, D]) for x in ("xp", "xf", "m", "h2n", "h2"))
        diag = n.sb("diag", [P, HALF, P])
        sq, x2, acc, y = (n.sb(x, [P, D]) for x in ("sq", "x2", "acc", "y"))
        h2T = n.sb("h2T", [P, DC, P])
        small = n.sb("small", [P, 8])
        eps, ss, rt, rs, ssf, rtf, rsf = (small[:, i:i + 1] for i in range(7))
        qn, qT, sc, sc2 = (n.sb(x, [P, K2]) for x in ("qn", "qT", "sc", "sc2"))
        v12, i12 = n.sb("v12", [P, 2, TOPK]), n.sb("i12", [P, 2, TOPK], U32)
        cand, cand2 = n.sb("cand", [P, TOPK, TOPK]), n.sb("cand2", [P, TOPK, TOPK])
        best, pos, ab = n.sb("best", [P, TOPK]), n.sb("pos", [P, TOPK], U32), n.sb("ab", [P, 2, TOPK], U32)
        eq, pick, sel = (n.sb("eq", [P, 2, TOPK, TOPK]), n.sb("pick", [P, 2, TOPK, TOPK]), n.sb("sel", [P, 2, TOPK]))
        iota = n.sb("iota", [P, TOPK])
        nbest, eg, dg, rg = n.sb("nbest", [P, 1]), n.sb("eg", [P, TOPK]), n.sb("dg", [P, 1]), n.sb("rg", [P, 1])
        gates = n.sb("gates", [P, 2, TOPK])
        idx_u, idx_v = n.sb("idx_u", [P, 2, TOPK], U32), n.sb("idx_v", [P, 2, TOPK], U32)
        act_, g1, g2, g3, g4 = (n.sb(x, [P, TOPK]) for x in ("act", "g1", "g2", "g3", "g4"))
        coef = n.sb("coef", [P, 2, TOPK])
        rows_u, rows_v = n.sb("rows_u", [P, U, D]), n.sb("rows_v", [P, 2, V2, D])
        psT = n.ps("psT", [P, DC * P])
        psA = n.ps("psA", [P, D])
        psQ, psQT, psS = n.ps("psQ", [P, 512]), n.ps("psQT", [P, 512]), n.ps("psS", [P, 512])

        const_in, row_in, gate_in = n.sem("const_loaded"), n.sem("rows_loaded"), n.sem("gate_loaded")
        xp_in, xf_in, stored = n.sem("xp_loaded"), n.sem("xf_loaded"), n.sem("stored")
        sk_turned, eps_set = n.sem("sk_turned"), n.sem("eps_set")
        squared, rooted, scaled, shifted = n.sem("squared"), n.sem("rooted"), n.sem("scaled"), n.sem("shifted")
        turned, hT_kept = n.sem("turned"), n.sem("hT_kept")
        q_done, q_kept, qt_done, qt_kept = n.sem("q"), n.sem("q_kept"), n.sem("qt"), n.sem("qt_kept")
        s_done, s_kept = n.sem("s"), n.sem("s_kept")
        pool_passed, pe_passed, dve_passed = n.sem("pool_passed"), n.sem("pe_passed"), n.sem("dve_passed")
        best_neg, gate_exp, gate_used = n.sem("best_neg"), n.sem("gate_exp"), n.sem("gate_used")
        u_named, v_named = n.sem("u_named"), n.sem("v_named")
        u_in, v_in = n.sems("u_in", U), [n.sems("v_even_in", V2), n.sems("v_odd_in", V2)]
        u_free, v_even_free, v_odd_free = n.sem("u_free"), n.sem("v_even_free"), n.sem("v_odd_free")
        coef_set, diag_set, acc_read = n.sem("coef_set"), n.sem("diag_set"), n.sem("acc_read")
        gelu_in, gelu_exp = n.sem("gelu_in"), n.sem("gelu_exp")
        x2_done, f_squared, f_rooted, y_done = n.sem("x2"), n.sem("f_squared"), n.sem("f_rooted"), n.sem("y_done")
        own, folded = n.sem("own"), n.sem("folded")
        ident = keep["ident"]
        block = ctx.enter_context(nc.Block())

        def x1_rows(t, R):
            return io["x1"][bass.ds(t * P, R), :]

        def is_sample(t):
            return isinstance(t, int) and t == PT

        def experts_of(t):
            return TOPK // 2 if is_sample(t) else TOPK

        def experts_before(t, kind):
            if isinstance(t, int) and t == 0 and kind == 0:
                return 0
            return TOPK // 2 if is_sample(t) and kind else TOPK

        def experts_next(t):
            if isinstance(t, int) and t >= PT - 1:
                return TOPK // 2 if t == PT - 1 else 0
            return TOPK

        def experts_of_job(t, kind, ahead):
            return experts_next(t) if kind + ahead >= HEADS else experts_of(t)

        def before(s, E, of=1):
            return TOPK // of * s if E == TOPK else TOPK // 2 // of * (s + PT * HEADS)

        def landed(s, E, slot):
            return 2 * s + slot + 1 if E == TOPK else s + PT * HEADS + 1

        def walk(eng, step):
            def tile(t):
                step(t, 0, 0, 0)
                step(t, 1, 1, 1)
                with eng.Fori(1, 3) as p:
                    step(t, 2, 2 * p, 0)
                    step(t, 3, 2 * p + 1, 1)
                step(t, 6, 6, 0)
                step(t, 7, 7, 1)

            tile(0)
            with eng.Fori(1, PT - 1) as t:
                tile(t)
            tile(PT - 1)
            tile(PT)

        @block.sync
        def _(sp):
            twice = bass.AP(io["x1"].tensor, io["x1"].offset + SEQ * D, [[0, 2], [D, NS], [1, D]])

            def tile(t, R, after=None):
                if after:
                    sp.wait_ge(scaled, t + 1)
                    sp.dma_start(xp[:], x1_rows(t + 1, P) if after == P else twice).then_inc(xp_in, 16)
                if not isinstance(t, int) or t:
                    sp.wait_ge(y_done, t)
                    sp.dma_start(io["y_prompt"][bass.ds((t - 1) * P, P), :], y[:]).then_inc(stored, 16)
                sp.dma_start(xf[0:R, :], x1_rows(t, R)).then_inc(xf_in, 16)

            sp.dma_start(xp[:], x1_rows(0, P)).then_inc(xp_in, 16)
            load_rows(sp, io, gain, 0, 4 * D, row_in)
            load_rows(sp, io, shift, 0, 3 * D, row_in)
            sp.dma_start(sk[:], io["sub_keys"].rearrange("s k d -> k s d")).then_inc(const_in, 16)
            sp.dma_start(iota[:], io["iota16"]).then_inc(const_in, 16)
            load_rows(sp, io, gate2, 0, 5 * D, gate_in)
            sp.dma_start(gainf[:], io["norm_f_g"].broadcast_to([P, D])).then_inc(gate_in, 16)
            tile(0, P, P)
            with sp.Fori(1, PT - 1) as t:
                tile(t, P, P)
            sp.wait_ge(shifted, PT)
            for i in (0, NS):
                load_rows(sp, io, gain[i:i + NS, :], PT, 4 * D, row_in)
                load_rows(sp, io, shift[i:i + NS, :], PT, 3 * D, row_in)
            tile(PT - 1, P, NS)
            sp.wait_ge(y_done, PT)
            load_rows(sp, io, gate2, PT, 5 * D, gate_in)
            tile(PT, NS)
            sp.wait_ge(y_done, NT)
            sp.dma_start(io["y_sample"], y[0:NS, :]).then_inc(stored, 16)
            sp.wait_ge(stored, 16 * NT)

        @block.gpsimd
        def _(pool):
            pool.memset(eps, EPS).then_inc(eps_set, 1)
            passed = pool_passed

            def gather(table, idx, k, dst, loaded):
                pool.indirect_dma_start(
                    out=dst, out_offset=None, in_=table,
                    in_offset=bass.IndirectOffsetOnAxis(ap=idx[:, k:k + 1], axis=0)).then_inc(loaded, 16)

            def step(s, b, EU, EV):
                for i in range(TOPK // 4):
                    if 4 * i < EU:
                        if i == 0:
                            wait_apart(pool, u_named, s + 1, passed)
                        wait_apart(pool, u_free, before(s, EU) + 4 * i + 4, passed)
                        for k in range(4 * i, 4 * i + 4):
                            gather(io["expert_u"], idx_u[:, b], k, rows_u[:, k % U, :], u_in[k % U])
                    if 4 * i < EV:
                        if i == 0:
                            wait_apart(pool, v_named, s, passed)
                        wait_apart(pool, v_even_free, before(s - 1, EV, 2) + 2 * i + 2, passed)
                        wait_apart(pool, v_odd_free, before(s - 1, EV, 2) + 2 * i + 2, passed)
                        for k in range(4 * i, 4 * i + 4):
                            gather(io["expert_v"], idx_v[:, 1 - b], k,
                                   rows_v[:, k % 2, k // 2 % V2, :], v_in[k % 2][k // 2 % V2])

            S0, ES = PT * HEADS, TOPK // 2
            step(0, 0, TOPK, 0)
            step(1, 1, TOPK, TOPK)
            with pool.Fori(1, S0 // 2) as q:
                step(2 * q, 0, TOPK, TOPK)
                step(2 * q + 1, 1, TOPK, TOPK)
            step(S0, 0, ES, TOPK)
            step(S0 + 1, 1, ES, ES)
            with pool.Fori(S0 // 2 + 1, LAST // 2) as q:
                step(2 * q, 0, ES, ES)
                step(2 * q + 1, 1, ES, ES)
            step(LAST, 0, 0, ES)

        @block.tensor
        def _(pe):
            def wait(sem, value):
                wait_apart(pe, sem, value, pe_passed)

            def turn(t):
                wait(shifted, t + 1)
                for k in range(DC):
                    last = pe.transpose(psT[:, k * P:(k + 1) * P], h2n[:, k * P:(k + 1) * P], ident[:])
                last.then_inc(turned, 1)

            def query(j, h):
                wait(s_kept, j + 1)
                for k in range(DC):
                    last = pe.matmul(psQ[:, 0:KD], h2T[:, k, :], wq[:, k, bass.ds(h * KD, KD)],
                                     start=(k == 0), stop=(k == DC - 1))
                last.then_inc(q_done, 1)
                wait(q_kept, j + 1)
                for i in range(2):
                    last = pe.transpose(psQT[:, i * P:(i + 1) * P], qn[:, i * P:(i + 1) * P], ident[:])
                last.then_inc(qt_done, 1)
                wait(qt_kept, j + 1)
                for i in range(2):
                    last = pe.matmul(psS[:, i * KEYS:(i + 1) * KEYS], qT[:, i * P:(i + 1) * P], skT[:, i, :],
                                     start=True, stop=True)
                last.then_inc(s_done, 1)

            pe.wait_ge(const_in, 32)
            for i in range(2):
                last = pe.transpose(psQ[:, i * P:(i + 1) * P], sk[:, i, :], ident[:])
            last.then_inc(sk_turned, 1)

            def add_row(s, i, E, first):
                wait(diag_set, before(s, E, 2) + i + 1)
                wait(v_in[1][i % V2], 16 * landed(s, E, i // V2))
                for c in range(2):
                    last = pe.matmul(psA[:, c * 512:(c + 1) * 512], diag[:, i, :],
                                     rows_v[:, 1, i % V2, c * 512:(c + 1) * 512],
                                     start=(first and i == 0), stop=False, skip_group_check=True)
                last.then_inc(v_odd_free, 1)

            def step(t, kind, h, b):
                s = t * HEADS + h
                EV = experts_before(t, kind)
                first = kind == 1
                if first and not (isinstance(t, int) and t == 0):
                    wait(acc_read, t)
                for i in range(EV // 4):
                    add_row(s - 1, i, EV, first)
                if kind == 6 and experts_next(t):
                    turn(t + 1)
                    wait(hT_kept, 2 * (t + 2))
                if experts_of_job(t, kind, 2):
                    query(s + 2, h + 2 if kind < 6 else kind - 6)
                for i in range(EV // 4, EV // 2):
                    add_row(s - 1, i, EV, first)

            turn(0)
            pe.wait_ge(hT_kept, 2)
            query(0, 0)
            query(1, 1)
            walk(pe, step)
            ES = experts_of(PT)
            for i in range(ES // 2):
                add_row(LAST - 1, i, ES, False)
            pe.wait_ge(acc_read, NT)
            for c in range(2):
                for i in range(2):
                    last = pe.matmul(psA[0:NS, c * 512:(c + 1) * 512], ident[:, i * NS:(i + 1) * NS],
                                     acc[:, c * 512:(c + 1) * 512], start=(i == 0), stop=(i == 1))
            last.then_inc(folded, 1)

        @block.scalar
        def _(act):
            def prep(t):
                act.wait_ge(xp_in, 16 * (t + 1))
                act.activation(sq[:], xp[:], ACT.Square, accum_out=ss).then_inc(squared, 1)
                act.wait_ge(squared, t + 1)
                act.activation(rt, ss, ACT.Sqrt, bias=eps, scale=1.0 / D).then_inc(rooted, 1)
                act.wait_ge(turned, t + 1)
                for i in range(2):
                    src = psT[:, i * 512:(i + 1) * 512].rearrange("p (c r) -> p c r", r=P)
                    act.activation(h2T[:, 4 * i:4 * i + 4, :], src, ACT.Copy).then_inc(hT_kept, 1)

            def scores(j):
                act.wait_ge(q_done, j + 1)
                act.activation(qn[:], psQ[:, 0:KD], ACT.Copy).then_inc(q_kept, 1)
                act.wait_ge(qt_done, j + 1)
                act.activation(qT[:], psQT[:, 0:2 * P], ACT.Copy).then_inc(qt_kept, 1)
                act.wait_ge(s_done, j + 1)
                if not isinstance(j, int) or j:
                    act.wait_ge(best_neg, j)
                act.activation(sc[:], psS[:, 0:K2], ACT.Copy).then_inc(s_kept, 1)

            def gate(j):
                act.wait_ge(best_neg, j + 1)
                if not isinstance(j, int) or j:
                    act.wait_ge(gate_used, j)
                act.activation(eg[:], best[:], ACT.Exp, bias=nbest[:], accum_out=dg[:]).then_inc(gate_exp, 1)

            def final(t, R):
                act.wait_ge(x2_done, t + 1)
                act.activation(sq[0:R, :], x2[0:R, :], ACT.Square, accum_out=ssf[0:R, :]).then_inc(f_squared, 1)
                act.wait_ge(f_squared, t + 1)
                act.activation(rtf[0:R, :], ssf[0:R, :], ACT.Sqrt, bias=eps[0:R, :],
                               scale=1.0 / D).then_inc(f_rooted, 1)

            def spread(s, b, E):
                act.wait_ge(coef_set, s + 1)
                for i in range(E // 2):
                    if i == 0 and not (isinstance(s, int) and s == 0):
                        act.wait_ge(v_odd_free, V2 + before(s, E, 2))
                    act.activation(diag[:, i, :], ident[:], ACT.Copy,
                                   scale=coef[:, b, 2 * i + 1:2 * i + 2]).then_inc(diag_set, 1)

            def step(t, kind, h, b):
                s = t * HEADS + h
                E = experts_of(t)
                if experts_before(t, kind):
                    spread(s - 1, 1 - b, experts_before(t, kind))
                if experts_of_job(t, kind, 1):
                    gate(s + 1)
                if kind == 6 and experts_next(t):
                    prep(t + 1)
                if experts_of_job(t, kind, 2):
                    scores(s + 2)
                act.wait_ge(gelu_in, s + 1)
                act.activation(g4[:, 0:E], g3[:, 0:E], ACT.Exp, scale=-GELU).then_inc(gelu_exp, 1)
                if kind == 0 and not (isinstance(t, int) and t == 0):
                    final(t - 1, P)

            act.wait_ge(eps_set, 1)
            act.wait_ge(sk_turned, 1)
            act.activation(skT[:].rearrange("p i k -> p (i k)"), psQ[:, 0:2 * P], ACT.Copy).then_inc(s_kept, 1)
            prep(0)
            scores(0)
            gate(0)
            scores(1)
            walk(act, step)
            spread(LAST - 1, 1, experts_of(PT))
            final(PT, NS)

        @block.vector
        def _(dve):
            link = Link(dve, own)

            def prep(t):
                dve.wait_ge(row_in, 96 if is_sample(t) else 32)
                dve.wait_ge(rooted, t + 1)
                link(dve.reciprocal(rs, rt))
                link.wait()
                dve.scalar_tensor_tensor(out=m[:], in0=xp[:], scalar=rs, in1=gain[:],
                                         op0=ALU.mult, op1=ALU.mult).then_inc(scaled, 1)
                dve.wait_ge(scaled, t + 1)
                dve.tensor_tensor(h2n[:], m[:], shift[:], ALU.add).then_inc(shifted, 1)

            def experts(j, b, E):
                def halves(f):
                    for i in range(2):
                        f(i, sc[:, i * KEYS:(i + 1) * KEYS], sc2[:, i * KEYS:(i + 1) * KEYS])
                    link.wait()

                wait_apart(dve, s_kept, j + 2, dve_passed)
                halves(lambda i, a, b: link(dve.max(v12[:, i, 0:8], a)))

                def second(i, a, b):
                    link(dve.max_index(i12[:, i, 0:8], v12[:, i, 0:8], a))
                    link(dve.match_replace(b, v12[:, i, 0:8], a, LOW))

                halves(second)
                halves(lambda i, a, b: link(dve.max(v12[:, i, 8:16], b)))
                halves(lambda i, a, b: link(dve.max_index(i12[:, i, 8:16], v12[:, i, 8:16], b)))
                c, c2 = (x[:].rearrange("p a b -> p (a b)") for x in (cand, cand2))
                link(dve.tensor_tensor(cand[:], v12[:, 0, :].unsqueeze(2).broadcast_to([P, TOPK, TOPK]),
                                       v12[:, 1:2, :].broadcast_to([P, TOPK, TOPK]), ALU.add))
                link.wait()
                link(dve.max(best[:, 0:8], c))
                link.wait()
                link(dve.max_index(pos[:, 0:8], best[:, 0:8], c))
                link(dve.match_replace(c2, best[:, 0:8], c, LOW))
                link.wait()
                link(dve.max(best[:, 8:16], c2))
                link.wait()
                dve.tensor_scalar(nbest[:, :], best[:, 0:1], -1.0, None, ALU.mult).then_inc(best_neg, 1)
                link(dve.max_index(pos[:, 8:16], best[:, 8:16], c2))
                link.wait()
                link(dve.tensor_scalar(ab[:, 0, :], pos[:, :], 4, None, ALU.logical_shift_right))
                link(dve.tensor_scalar(ab[:, 1, :], pos[:, :], 15, None, ALU.bitwise_and))
                link.wait()
                shape = [P, 2, TOPK, TOPK]
                link(dve.tensor_tensor(eq[:], ab[:].unsqueeze(3).broadcast_to(shape),
                                       iota[:].unsqueeze(1).unsqueeze(1).broadcast_to(shape), ALU.is_equal))
                link.wait()
                link(dve.tensor_tensor(pick[:], eq[:], i12[:].unsqueeze(2).broadcast_to(shape), ALU.mult))
                link.wait()
                link(dve.tensor_reduce(sel[:], pick[:], AX, ALU.add))
                link.wait()
                parts = [(0, P, 0)] if E == TOPK else [(0, NS, 0), (NS, P, E)]
                for lo, hi, k in parts:
                    last = dve.scalar_tensor_tensor(out=idx_u[lo:hi, b, 0:E], in0=sel[lo:hi, 0, k:k + E],
                                                    scalar=float(KEYS), in1=sel[lo:hi, 1, k:k + E],
                                                    op0=ALU.mult, op1=ALU.add)
                    if hi < P:
                        link(last)
                        link.wait()
                last.then_inc(u_named, 1)
                dve.wait_ge(gate_exp, j + 1)
                link(dve.reciprocal(rg[:, :], dg[:, :]))
                link.wait()
                for lo, hi, k in parts:
                    last = dve.tensor_scalar(gates[lo:hi, b, 0:E], eg[lo:hi, k:k + E], rg[lo:hi, :], None, ALU.mult)
                    if hi < P:
                        link(last)
                        link.wait()
                last.then_inc(gate_used, 1)

            def final(t, R):
                added = before(HEADS * (t + 1), experts_of(t), 2)
                dve.wait_ge(v_even_free, V2 + added)
                dve.wait_ge(v_odd_free, V2 + added)
                dve.tensor_tensor(acc[:], acc[:], psA[:], ALU.add).then_inc(acc_read, 1)
                total = acc
                if is_sample(t):
                    dve.wait_ge(folded, 1)
                    total = psA
                else:
                    dve.wait_ge(acc_read, t + 1)
                dve.wait_ge(gate_in, 32 if R == P else 48)
                link(dve.tensor_tensor(m[0:R, :], total[0:R, :], gate2[0:R, :], ALU.mult))
                link.wait()
                dve.wait_ge(xf_in, 16 * (t + 1))
                dve.tensor_tensor(x2[0:R, :], m[0:R, :], xf[0:R, :], ALU.add).then_inc(x2_done, 1)
                dve.wait_ge(f_rooted, t + 1)
                link(dve.reciprocal(rsf[0:R, :], rtf[0:R, :]))
                link.wait()
                if not isinstance(t, int) or t:
                    dve.wait_ge(stored, 16 * t)
                dve.scalar_tensor_tensor(out=y[0:R, :], in0=x2[0:R, :], scalar=rsf[0:R, :], in1=gainf[0:R, :],
                                         op0=ALU.mult, op1=ALU.mult).then_inc(y_done, 1)

            def dot(s, k, E):
                dve.wait_ge(u_in[k % U], 16 * landed(s, E, k // U))
                dve.tensor_tensor_reduce(rows_u[:, k % U, :], rows_u[:, k % U, :], h2[:, :], 1.0, 0.0,
                                         ALU.mult, ALU.add, act_[:, k:k + 1]).then_inc(u_free, 1)

            def add_row(s, i, E, b, first):
                if i == 0:
                    dve.wait_ge(coef_set, s + 1)
                dve.wait_ge(v_in[0][i % V2], 16 * landed(s, E, i // V2))
                c = coef[:, b, 2 * i:2 * i + 1]
                if first:
                    dve.tensor_scalar(acc[:, :], rows_v[:, 0, i % V2, :], c, None,
                                      ALU.mult).then_inc(v_even_free, 1)
                    return
                dve.wait_ge(v_even_free, V2 + before(s, E, 2) + i)
                dve.scalar_tensor_tensor(out=acc[:, :], in0=rows_v[:, 0, i % V2, :], scalar=c,
                                         in1=acc[:, :], op0=ALU.mult, op1=ALU.add).then_inc(v_even_free, 1)

            def coefs(s, E, EB, b):
                a = act_[:, 0:E]
                dve.wait_ge(u_free, U + before(s, E) + E)
                link(dve.tensor_tensor(g1[:, 0:E], a, a, ALU.mult))
                link.wait()
                link(dve.tensor_scalar(g2[:, 0:E], g1[:, 0:E], 0.044715, 1.0, ALU.mult, ALU.add))
                link.wait()
                link(dve.tensor_tensor(g1[:, 0:E], g2[:, 0:E], a, ALU.mult))
                link.wait()
                dve.tensor_scalar(g3[:, 0:E], g1[:, 0:E], -50.0, None, ALU.max).then_inc(gelu_in, 1)
                dve.wait_ge(gelu_exp, s + 1)
                link(dve.tensor_scalar(g1[:, 0:E], g4[:, 0:E], 1.0, None, ALU.add))
                link.wait()
                link(dve.reciprocal(g2[:, 0:E], g1[:, 0:E]))
                link.wait()
                link(dve.tensor_tensor(g1[:, 0:E], g2[:, 0:E], a, ALU.mult))
                link.wait()
                if not isinstance(s, int) or s >= 2:
                    dve.wait_ge(diag_set, before(s - 1, EB, 2))
                dve.tensor_tensor(coef[:, b, 0:E], g1[:, 0:E], gates[:, b, 0:E], ALU.mult).then_inc(coef_set, 1)

            def step(t, kind, h, b):
                s = t * HEADS + h
                at = isinstance(t, int)
                E, EB, E1 = experts_of(t), experts_before(t, kind), experts_of_job(t, kind, 1)
                if kind == 0:
                    dve.wait_ge(u_free, U + before(s, E))
                    dve.wait_ge(shifted, t + 1)
                    link(dve.tensor_copy(h2[:, :], h2n[:, :]))
                link.restart()
                if E1:
                    experts(s + 1, 1 - b, E1)
                dve.wait_ge(u_named, s + 1)
                if not isinstance(s, int) or s >= 2:
                    dve.wait_ge(v_odd_free, V2 + before(s - 1, EB, 2))
                dve.tensor_copy(idx_v[:, b, 0:E], idx_u[:, b, 0:E]).then_inc(v_named, 1)
                if kind == 6 and experts_next(t):
                    prep(t + 1)
                for k in range(TOPK):
                    if k < E:
                        dot(s, k, E)
                    if k % 2 == 0 and k < EB:
                        add_row(s - 1, k // 2, EB, 1 - b, kind == 1 and k == 0)
                coefs(s, E, EB, b)
                if kind == 0 and not (at and t == 0):
                    final(t - 1, P)

            dve.memset(coef[:], 0.0).then_inc(u_free, U)
            dve.memset(act_[:], 0.0).then_inc(v_even_free, V2)
            dve.memset(g4[:], 0.0).then_inc(v_odd_free, V2)
            dve.wait_ge(const_in, 32)
            prep(0)
            experts(0, 0, TOPK)
            walk(dve, step)
            ES = experts_of(PT)
            for i in range(ES // 2):
                add_row(LAST - 1, i, ES, 1, False)
            final(PT, NS)


def layer(nc, io):
    with ExitStack() as whole:
        Names.spent = []
        top = Names(nc, whole, "keep")
        keep = {"ident": top.sb("ident", [P, P])}
        low = top.sb("low", [P, DC * HEADS * KD])
        keep["wq"] = low[:].rearrange("p (c n) -> p c n", c=DC)
        at = 0

        def part(rows, c, m):
            nonlocal at
            at += c * m
            return low[0:rows, at - c * m:at].rearrange("p (c m) -> p c m", c=c)

        keep["hT"], keep["oT"] = part(P, DC, TOK), part(P, 2, TOK)
        keep["spare"] = low[:, at:]
        keep["qTs"], keep["kTs"] = part(P, 6, NS), part(P, 6, NS)
        keep["Vs"] = low[0:NS, at:at + AW]
        with ExitStack() as front:
            ring = Names(nc, front, "front").sb("ring", [P, DC * D])
            SLOT = DC * WQKV
            keep["w_conv"] = ring[:, 0:2 * DC * 3 * P].rearrange("p (s c q m) -> p s c q m", s=2, c=DC, q=3)
            keep["w_ada"] = ring[:].rearrange("p (s c m) -> p s c m", s=2, c=DC)
            keep["pT"] = ring[:, 0:4 * 512].rearrange("p (r c) -> p r c", r=4)
            keep["w_out"] = ring[:].rearrange("p (c n) -> p c n", c=DC)
            with ExitStack() as prompt:
                p = Names(nc, prompt, "prompt")
                keep["mask"], keep["identb"] = p.sb("mask", [P, NMASK * P], BF16), p.sb("identb", [P, P], BF16)
                third = p.sb("third_slot", [P, SLOT])
                keep["w_qkv"] = [third[:], ring[:, 0:SLOT], ring[:, SLOT:2 * SLOT]]
                with ExitStack() as rows:
                    m = Names(nc, rows, "modulation")
                    keep["cT"], keep["mod"] = m.sb("cT", [P, DC, NQ]), m.sb("rows", [NQ, 6 * D])
                    keep["gains"] = m.sb("gains", [NQ, 2, D])
                    ada(nc, io, keep)
                    norm(nc, io, keep)
                keep["qT"], keep["kT"] = p.sb("qT", [P, 6, SEQ]), p.sb("kT", [P, 6, SEQ])
                keep["V"] = p.sb("V", [P, PT, AW])
                qkv(nc, io, keep)
                attend(nc, io, keep)
            sampled(nc, io, keep)
            Names.recycle(nc)
            with ExitStack() as branches:
                b = Names(nc, branches, "branches")
                keep["mT"], keep["tail"] = b.sb("mT", [P, DC, TOK]), b.sb("tail", [P, CT, TAIL])
                with ExitStack() as z:
                    zn = Names(nc, z, "z")
                    keep["zT"], keep["w_mix"] = zn.sb("zT", [P, CT, TOK]), zn.sb("w_mix", [P, 2, sum(KC), P])
                    conv(nc, io, keep)
                    mix(nc, io, keep)
                out(nc, io, keep)
        peer(nc, io, keep)


def kernel(x_prompt, x_sample, cache_kv0, cache_kv1, cache_kv2, state_conv, c_prompt, c_sample, norm1_g, norm2_g,
           norm_f_g, w_ada, b_ada, w_in, conv_w, w_attn_o, w_conv_o, w_o, w_query, sub_keys, expert_u, expert_v):
    import concourse.bacc as bacc
    from concourse.bass_utils import run_bass_kernel_spmd

    a = {
        "x_prompt": x_prompt[0], "x_sample": x_sample.reshape(NS, D), "state_conv": state_conv.reshape(2 * NSEQ, CW),
        "c_prompt": c_prompt, "c_sample": c_sample, "norm1_g": norm1_g, "norm2_g": norm2_g,
        "norm_f_g": norm_f_g.reshape(1, D), "w_ada": w_ada[0], "b_ada": b_ada, "w_in": w_in[0], "conv_w": conv_w[0],
        "w_attn_o": w_attn_o[0], "w_conv_o": w_conv_o[0], "w_o": w_o[0], "w_query": w_query[0],
        "sub_keys": sub_keys[0], "expert_u": expert_u[0], "expert_v": expert_v[0],
    }
    for g, c in enumerate((cache_kv0, cache_kv1, cache_kv2)):
        a[f"cache{g}"] = c[0].reshape(NSEQ, CACHE[g], 2, SLOTS * HD)
    a.update(constants())
    a = {k: np.ascontiguousarray(v) for k, v in a.items()}
    nc = bacc.Bacc("TRN2", target_bir_lowering=False, num_devices=1)
    io = {k: nc.dram_tensor(f"in_{k}", v.shape, F32, kind="ExternalInput").ap() for k, v in a.items()}
    io["cache"] = [io[f"cache{g}"] for g in range(GROUPS)]
    outs = []

    def output(shape):
        outs.append(f"out_{len(outs)}")
        return nc.dram_tensor(outs[-1], shape, F32, kind="ExternalOutput").ap()

    io["y_prompt"], io["y_sample"] = output((SEQ, D)), output((NS, D))
    io["kvp"] = [output((min(w, SEQ), 2, SLOTS * HD)) for w in WINDOWS]
    io["conv_prompt"] = output((2, CW))
    io["kvs"] = [output((NS, 2, SLOTS * HD)) for _ in WINDOWS]
    io["conv_sample"] = output((2 * NSEQ, CW))
    io["mod"] = nc.dram_tensor("mod_rows", (1 + NSEQ, 6 * D), F32, kind="Internal").ap()
    io["x1"] = nc.dram_tensor("x_after_mixing", (TOK, D), F32, kind="Internal").ap()
    layer(nc, io)
    got = run_bass_kernel_spmd(nc, [{f"in_{k}": v for k, v in a.items()}], core_ids=[0]).results[0]
    shapes = ([(1, SEQ, D), (NSEQ, NEW, D)] + [(1, 1, min(w, SEQ), 2, SLOTS, HD) for w in WINDOWS] + [(1, 1, 2, CW)]
              + [(1, NSEQ, NEW, 2, SLOTS, HD)] * GROUPS + [(1, NSEQ, 2, CW)])
    return tuple(got[n].reshape(s) for n, s in zip(outs, shapes))
```
